# Optimizing a Trainium2 kernel written in Bass

```python
import jax, jax.numpy as jnp
from jax import lax
import numpy as np

D_MODEL = 2048
BATCH = 1
SEQ = 512
DEPTH = 1

MEM_LEN = 256
HEAD_DIM = 128
N_CONV_GROUPS = 4
CONV_W = N_CONV_GROUPS * HEAD_DIM
CONV_K = 31
N_FOX_HEADS = 8
FOX_W = N_FOX_HEADS * HEAD_DIM
N_MEM_HEADS = 4
MEM_W = N_MEM_HEADS * HEAD_DIM
MIX_W = CONV_W + FOX_W + MEM_W
Q_BLOCK = 128
EPS = 1e-6
FORGET_BIAS_INIT = 2.0

SPLITS = (
    CONV_W,
    2 * CONV_W,
    3 * CONV_W,
    3 * CONV_W + FOX_W,
    3 * CONV_W + 2 * FOX_W,
    3 * CONV_W + 3 * FOX_W,
    3 * CONV_W + 3 * FOX_W + N_FOX_HEADS,
    3 * CONV_W + 4 * FOX_W + N_FOX_HEADS,
    3 * CONV_W + 4 * FOX_W + N_FOX_HEADS + MEM_W,
)
D_IN = 3 * CONV_W + 4 * FOX_W + N_FOX_HEADS + 2 * MEM_W


def rmsnorm(x, g):
    xf = x.astype(jnp.float32)
    y = xf * lax.rsqrt(jnp.mean(xf * xf, axis=-1, keepdims=True) + EPS)
    return (y * g.astype(jnp.float32)).astype(x.dtype)

def layernorm(x, g, b):
    xf = x.astype(jnp.float32)
    mu = jnp.mean(xf, axis=-1, keepdims=True)
    var = jnp.mean(jnp.square(xf - mu), axis=-1, keepdims=True)
    y = (xf - mu) * lax.rsqrt(var + EPS)
    return (y * g.astype(jnp.float32) + b.astype(jnp.float32)).astype(x.dtype)

def causal_depthwise_conv(u, w, b):
    y = lax.conv_general_dilated(
        u, w[:, None, :], window_strides=(1,), padding=[(CONV_K - 1, 0)],
        dimension_numbers=('NWC', 'WIO', 'NWC'), feature_group_count=u.shape[-1])
    return y + b

def fox_attention(q, k, v, logf):
    B, S, H, Dh = q.shape
    nb = S // Q_BLOCK
    cT = jnp.cumsum(logf, axis=1).transpose(0, 2, 1)
    qb = q.reshape(B, nb, Q_BLOCK, H, Dh).transpose(1, 0, 2, 3, 4)
    cb = cT.reshape(B, H, nb, Q_BLOCK).transpose(2, 0, 1, 3)
    k_pos = jnp.arange(S)
    scale = Dh ** -0.5

    def block(args):
        i, qi, ci = args
        s = jnp.einsum('bqhd,bkhd->bhqk', qi, k).astype(jnp.float32) * scale
        bias = ci[..., :, None] - cT[..., None, :]
        q_pos = i * Q_BLOCK + jnp.arange(Q_BLOCK)
        mask = k_pos[None, :] <= q_pos[:, None]
        s = jnp.where(mask, s + bias, -jnp.inf)
        p = jax.nn.softmax(s, axis=-1).astype(v.dtype)
        return jnp.einsum('bhqk,bkhd->bqhd', p, v)

    out = lax.map(block, (jnp.arange(nb), qb, cb))
    return out.transpose(1, 0, 2, 3, 4).reshape(B, S, H * Dh)

def memory_attention(q, mk, mv):
    B, S, H, Dh = q.shape
    s = jnp.einsum('bshd,bmhd->bhsm', q, mk).astype(jnp.float32) * (Dh ** -0.5)
    p = jax.nn.softmax(s, axis=-1).astype(mv.dtype)
    return jnp.einsum('bhsm,bmhd->bshd', p, mv).reshape(B, S, H * Dh)

def first_inputs(seed: int = 0) -> dict:
    key = jax.random.key(seed)
    ks = jax.random.split(key, 16)
    n = jax.random.normal
    f32 = jnp.float32
    return {
        "x": n(ks[0], (BATCH, SEQ, D_MODEL), f32),
        "mem": n(ks[1], (BATCH, MEM_LEN, D_MODEL), f32),
        "norm_g": 1.0 + 0.05 * n(ks[2], (DEPTH, D_MODEL), f32),
        "mem_norm_g": 1.0 + 0.05 * n(ks[3], (DEPTH, D_MODEL), f32),
        "w_in": n(ks[4], (DEPTH, D_MODEL, D_IN), f32) * D_MODEL ** -0.5,
        "b_f": FORGET_BIAS_INIT + 0.1 * n(ks[5], (DEPTH, N_FOX_HEADS), f32),
        "conv_w": n(ks[6], (DEPTH, CONV_K, CONV_W), f32) * CONV_K ** -0.5,
        "conv_b": 0.02 * n(ks[7], (DEPTH, CONV_W), f32),
        "conv_ln_g": 1.0 + 0.05 * n(ks[8], (DEPTH, CONV_W), f32),
        "conv_ln_b": 0.02 * n(ks[9], (DEPTH, CONV_W), f32),
        "w_conv_pw": n(ks[10], (DEPTH, CONV_W, CONV_W), f32) * CONV_W ** -0.5,
        "w_mem_kv": n(ks[11], (DEPTH, D_MODEL, 2 * MEM_W), f32) * D_MODEL ** -0.5,
        "w_out": n(ks[12], (DEPTH, MIX_W, D_MODEL), f32) * MIX_W ** -0.5,
        "final_g": 1.0 + 0.05 * n(ks[13], (D_MODEL,), f32),
    }

def first_block(x, mem, norm_g, mem_norm_g, w_in, b_f, conv_w, conv_b, conv_ln_g,
              conv_ln_b, w_conv_pw, w_mem_kv, w_out, final_g):
    B, S, _ = x.shape
    for l in range(DEPTH):
        h = rmsnorm(x, norm_g[l])
        proj = h @ w_in[l]
        (cv_a, cv_b, cv_gate, fq, fk, fv, f_logit, fox_gate,
         mq, mem_gate) = jnp.split(proj, SPLITS, axis=-1)

        u = cv_a * jax.nn.sigmoid(cv_b)
        u = causal_depthwise_conv(u, conv_w[l], conv_b[l])
        u = jax.nn.silu(layernorm(u, conv_ln_g[l], conv_ln_b[l]))
        y_conv = (u @ w_conv_pw[l]) * jax.nn.silu(cv_gate)

        logf = jax.nn.log_sigmoid(f_logit.astype(jnp.float32) + b_f[l].astype(jnp.float32))
        shp = (B, S, N_FOX_HEADS, HEAD_DIM)
        y_fox = fox_attention(fq.reshape(shp), fk.reshape(shp), fv.reshape(shp), logf)
        y_fox = y_fox * jax.nn.silu(fox_gate)

        mkv = rmsnorm(mem, mem_norm_g[l]) @ w_mem_kv[l]
        mk, mv = jnp.split(mkv, 2, axis=-1)
        mshp = (B, mem.shape[1], N_MEM_HEADS, HEAD_DIM)
        y_mem = memory_attention(mq.reshape(B, S, N_MEM_HEADS, HEAD_DIM),
                                 mk.reshape(mshp), mv.reshape(mshp))
        y_mem = y_mem * jax.nn.silu(mem_gate)

        y = jnp.concatenate([y_conv, y_fox, y_mem], axis=-1)
        x = x + y @ w_out[l]
    return rmsnorm(x, final_g)


CHUNK = 64
MIX_WIDTH = D_MODEL
ATT_WIDTH = MIX_WIDTH // 2
HG_WIDTH = MIX_WIDTH - ATT_WIDTH
ATT_HEAD_DIM = 128
ATT_HEADS = ATT_WIDTH // ATT_HEAD_DIM
ATT_LEFT_CHUNKS = 8
ATT_BAND = ATT_LEFT_CHUNKS + 1
MAX_REL = 128
HG_EXPAND = 128
HG_HEADS = HG_WIDTH // HG_EXPAND
HG_KDIM = HG_EXPAND
HG_FDIM = HG_HEADS * HG_KDIM
HG_VDIM = HG_WIDTH // HG_HEADS
IN_SPLITS = (ATT_WIDTH, ATT_WIDTH, ATT_WIDTH, ATT_WIDTH, HG_FDIM, HG_FDIM, HG_WIDTH, HG_WIDTH)
IN_COLS = sum(IN_SPLITS)


def _rms(x, g):
    xf = x.astype(jnp.float32)
    y = xf * lax.rsqrt(jnp.mean(xf * xf, axis=-1, keepdims=True) + EPS)
    return (y * g.astype(jnp.float32)).astype(x.dtype)

def _chunk_attention(q, k, v, q_g, k_g, rel_bias):
    B, T, H, dh = q.shape
    N = T // CHUNK
    q = _rms(q, q_g).reshape(B, N, CHUNK, H, dh)
    k = _rms(k, k_g).reshape(B, N, CHUNK, H, dh)
    v = v.reshape(B, N, CHUNK, H, dh)
    pad = ((0, 0), (ATT_LEFT_CHUNKS, 0), (0, 0), (0, 0), (0, 0))
    kp = jnp.pad(k, pad)
    vp = jnp.pad(v, pad)
    band_idx = jnp.arange(N)[:, None] + jnp.arange(ATT_BAND)[None, :]
    kb = kp[:, band_idx].reshape(B, N, ATT_BAND * CHUNK, H, dh)
    vb = vp[:, band_idx].reshape(B, N, ATT_BAND * CHUNK, H, dh)
    scores = jnp.einsum('bnqhd,bnkhd->bnhqk', q, kb).astype(jnp.float32) * (dh ** -0.5)
    qi = jnp.arange(CHUNK)
    kj = jnp.arange(ATT_BAND * CHUNK)
    dist = ATT_LEFT_CHUNKS * CHUNK + qi[:, None] - kj[None, :]
    bias_idx = jnp.clip(dist, -MAX_REL, MAX_REL) + MAX_REL
    bias = rel_bias.astype(jnp.float32)[:, bias_idx]
    valid = (jnp.arange(N)[:, None] + kj[None, :] // CHUNK) >= ATT_LEFT_CHUNKS
    scores = jnp.where(valid[None, :, None, None, :], scores + bias[None, None], -jnp.inf)
    p = jax.nn.softmax(scores, axis=-1).astype(v.dtype)
    out = jnp.einsum('bnhqk,bnkhd->bnqhd', p, vb)
    return out.reshape(B, T, H * dh)

def _hgrn2(q_raw, f_raw, i, lb, o_g):
    B, T, _ = q_raw.shape
    N = T // CHUNK
    out_dtype = i.dtype
    f32 = jnp.float32
    q = jax.nn.silu(q_raw.astype(f32))
    fr = f_raw.astype(f32)
    lb = lb.astype(f32)
    logf = jnp.log(lb + (1.0 - lb) * jax.nn.sigmoid(fr))
    k = (1.0 - lb) * jax.nn.sigmoid(-fr)
    v = i.astype(f32)

    def to_chunks(a, d):
        return a.reshape(B, N, CHUNK, HG_HEADS, d).transpose(1, 0, 3, 2, 4)

    qc, kc, lc = to_chunks(q, HG_KDIM), to_chunks(k, HG_KDIM), to_chunks(logf, HG_KDIM)
    vc = to_chunks(v, HG_VDIM)
    tril = jnp.arange(CHUNK)[:, None] >= jnp.arange(CHUNK)[None, :]

    def step(S, xs):
        qn, kn, vn, ln = xs
        b = jnp.cumsum(ln, axis=2)
        b_last = b[:, :, -1]
        inter = jnp.einsum('bhcd,bhde->bhce', qn * jnp.exp(b), S)
        diff = b[:, :, :, None, :] - b[:, :, None, :, :]
        decay = jnp.exp(jnp.where(tril[None, None, :, :, None], diff, -jnp.inf))
        A = jnp.einsum('bhtd,bhtsd,bhsd->bhts', qn, decay, kn)
        intra = jnp.einsum('bhts,bhse->bhte', A, vn)
        k_dec = kn * jnp.exp(b_last[:, :, None, :] - b)
        S_new = jnp.exp(b_last)[..., None] * S + jnp.einsum('bhsd,bhse->bhde', k_dec, vn)
        return S_new, inter + intra

    S0 = jnp.zeros((B, HG_HEADS, HG_KDIM, HG_VDIM), f32)
    _, o = lax.scan(step, S0, (qc, kc, vc, lc))
    o = o.transpose(1, 0, 3, 2, 4).reshape(B, T, HG_HEADS, HG_VDIM)
    o = _rms(o, o_g)
    return o.reshape(B, T, HG_WIDTH).astype(out_dtype)

def second_inputs(seed: int = 0) -> dict:
    key = jax.random.key(seed)
    ks = jax.random.split(key, 16)
    D = D_MODEL
    f32 = jnp.float32
    nrm = lambda k, s: jax.random.normal(k, s, f32)
    return {
        "x": nrm(ks[0], (BATCH, SEQ, D)),
        "c": nrm(ks[1], (BATCH, D)),
        "norm_g": 1.0 + 0.1 * nrm(ks[2], (DEPTH, D)),
        "w_ada": nrm(ks[3], (DEPTH, D, 3 * D)) * D ** -0.5,
        "b_ada": 0.01 * nrm(ks[4], (DEPTH, 3 * D)),
        "w_in": nrm(ks[5], (DEPTH, D, IN_COLS)) * D ** -0.5,
        "q_norm_g": 1.0 + 0.1 * nrm(ks[6], (DEPTH, ATT_HEAD_DIM)),
        "k_norm_g": 1.0 + 0.1 * nrm(ks[7], (DEPTH, ATT_HEAD_DIM)),
        "rel_bias": 0.5 * nrm(ks[8], (DEPTH, ATT_HEADS, 2 * MAX_REL + 1)),
        "lower_bounds": nrm(ks[9], (DEPTH + 1, HG_FDIM)),
        "hg_norm_g": 1.0 + 0.1 * nrm(ks[10], (DEPTH, HG_VDIM)),
        "w_out": nrm(ks[11], (DEPTH, MIX_WIDTH, D)) * MIX_WIDTH ** -0.5,
    }

def second_block(x, c, norm_g, w_ada, b_ada, w_in, q_norm_g, k_norm_g, rel_bias,
              lower_bounds, hg_norm_g, w_out):
    B, T, D = x.shape
    lbs = jnp.cumsum(jax.nn.softmax(lower_bounds.astype(jnp.float32), axis=0), axis=0)
    offsets = np.cumsum(IN_SPLITS)[:-1].tolist()
    c_act = jax.nn.silu(c)
    for l in range(DEPTH):
        mod = c_act @ w_ada[l] + b_ada[l]
        shift, scale, gate = jnp.split(mod, 3, axis=-1)
        h = _rms(x, norm_g[l]) * (1.0 + scale[:, None, :]) + shift[:, None, :]
        proj = h @ w_in[l]
        a_q, a_k, a_v, a_z, g_q, g_f, g_i, g_z = jnp.split(proj, offsets, axis=-1)
        hs = (B, T, ATT_HEADS, ATT_HEAD_DIM)
        att = _chunk_attention(a_q.reshape(hs), a_k.reshape(hs), a_v.reshape(hs),
                               q_norm_g[l], k_norm_g[l], rel_bias[l])
        att = att * jax.nn.silu(a_z)
        hg = _hgrn2(g_q, g_f, g_i, lbs[l], hg_norm_g[l]) * jax.nn.silu(g_z)
        y = jnp.concatenate([att, hg], axis=-1) @ w_out[l]
        x = x + gate[:, None, :] * y
    return x


def setup_inputs(seed=0):
    out = dict(first_inputs(seed))
    for name, value in second_inputs(seed + 1).items():
        if name != "x":
            out[name + "_2"] = value
    return out


def reference(
    x, mem, norm_g, mem_norm_g, w_in, b_f, conv_w, conv_b, conv_ln_g, conv_ln_b, w_conv_pw,
    w_mem_kv, w_out, final_g, c_2, norm_g_2, w_ada_2, b_ada_2, w_in_2, q_norm_g_2, k_norm_g_2,
    rel_bias_2, lower_bounds_2, hg_norm_g_2, w_out_2,
):
    x = first_block(
        x, mem, norm_g, mem_norm_g, w_in, b_f, conv_w, conv_b, conv_ln_g, conv_ln_b, w_conv_pw,
        w_mem_kv, w_out, final_g,
    )
    return second_block(
        x, c_2, norm_g_2, w_ada_2, b_ada_2, w_in_2, q_norm_g_2, k_norm_g_2, rel_bias_2,
        lower_bounds_2, hg_norm_g_2, w_out_2,
    )


_drawn_inputs = setup_inputs


def setup_inputs(seed=0):
    import zlib

    import numpy as np

    out = dict(_drawn_inputs(seed))
    spreads = {}
    factors = {'norm_g': 2.717,
     'mem_norm_g': 8.0,
     'b_f': 52.144,
     'conv_b': 7.751,
     'conv_ln_g': 5.496,
     'conv_ln_b': 8.0,
     'b_ada_2': 5.746,
     'q_norm_g_2': 8.0,
     'k_norm_g_2': 8.0,
     'rel_bias_2': 2.972,
     'lower_bounds_2': 2.842}
    for name, (base, spread) in spreads.items():
        noise = np.random.default_rng([zlib.crc32(name.encode()), seed]).standard_normal(out[name].shape)
        drawn = base * np.exp(spread * noise) if base else spread * noise
        out[name] = __import__('jax').numpy.asarray(drawn.astype(out[name].dtype))
    for name, factor in factors.items():
        out[name] = (out[name] * factor).astype(out[name].dtype)
    return out
```

```python
from contextlib import ExitStack

import concourse.bass as bass
from concourse import mybir

ALU = mybir.AluOpType
ACT = mybir.ActivationFunctionType
AX_X = mybir.AxisListType.X
F32 = mybir.dt.float32
F32R = mybir.dt.float32r
BF16 = mybir.dt.bfloat16
U16 = mybir.dt.uint16

P = 128
D = 2048
KT = D // P
S = 512
QT = S // P
MEM = 256
MT = MEM // P
CHUNK = 64
NCH = S // CHUNK
HALVES = (32, 16, 8, 4, 2, 1)
NLEV = len(HALVES) + 1
TAPS = 31
NCONV = 4
NMEMH = 4
NFOX = 8
NATT = 8
NHG = 8
ADA_COLS = 6 * P
EPS = 1e-6
SCALE = float(P) ** -0.5
LB_LEAST = 1e-19
NEG = -1e30

PHASES = {
    "start": (1, 0),
    "mem_a": (2, 2),
    "xnorm": (1, 0),
    "mem_b": (2, 2),
    "conv": (4, 2),
    "flog": (1, 1),
    "memh": (4, 2),
    "cums": (1, 0),
    "fox": (8, 4),
    "gate": (1, 4),
    "pw": (1, 0),
    "out1": (8, 2),
    "norm2": (1, 0),
    "att": (8, 4),
    "hg": (8, 4),
    "out2": (8, 2),
}
TILE0 = {}
_t = 0
for _name, (_n, _w) in PHASES.items():
    TILE0[_name] = _t
    _t += _n * _w
NTILES = _t

COLS = {}
_c = 0
for _name, _n in (("norm_g", 16), ("mem_norm_g", 16), ("final_g", 16), ("norm_g_2", 16), ("c_2", 16),
                  ("b_ada_2", 48), ("conv_w", NCONV * TAPS), ("conv_b", 4), ("conv_ln_g", 4), ("conv_ln_b", 4),
                  ("q_norm_g_2", 1), ("k_norm_g_2", 1), ("hg_norm_g_2", 1), ("lower_bounds_2", 16), ("b_f", 1),
                  ("one", 1), ("eps", 1)):
    COLS[_name] = (_c, _n)
    _c += _n
NCOLS = _c

CONSTS = 2 * P + S


class Count:

    def __init__(self, sem, **per):
        self.sem, self.base, self.per = sem, {}, {}
        n = 0
        for name, (iters, _) in PHASES.items():
            self.base[name], self.per[name] = n, per.get(name, 0)
            n += iters * per.get(name, 0)

    def at(self, phase, i, k):
        return self.per[phase] * i + (1 + self.base[phase] + k)


class Order:

    def __init__(self, eng, sem):
        self.eng, self.sem, self.n = eng, sem, 0

    def step(self, ins):
        self.n += 1
        ins.then_inc(self.sem, 1)

    def settle(self):
        if self.n:
            self.eng.wait_ge(self.sem, self.n)

    def note(self):
        self.n += 1
        self.eng.sem_inc(self.sem, 1)

    def again(self):
        self.eng.sem_clear(self.sem)
        self.n = 0


def build(nc, wt, ada, bias, xT, memT, pw, cols_d, consts_d, masks_d, spill, out):
    ctx = ExitStack()
    with ctx:
        def sb(name, shape, dt=F32, stack=ctx):
            return stack.enter_context(nc.sbuf_tensor(name, shape, dt))

        def sem(name):
            return ctx.enter_context(nc.semaphore(name))

        act_hi = sb("act_hi", [P, KT, S], F32R)
        act_lo = sb("act_lo", [P, KT, S], F32R)
        Y = sb("Y", [P, KT, S])
        raw = sb("raw", [P, 2, D])
        w_hi = sb("w_hi", [P, 2, D], F32R)
        w_lo = sb("w_lo", [P, 2, D], F32R)
        cols = sb("cols", [P, NCOLS])
        consts = sb("consts", [P, CONSTS])
        masks = sb("masks", [P, 3 + NLEV, P], BF16)
        levels = masks[:, 3:3 + NLEV, :].bitcast(U16)
        mod = sb("mod", [P, 48])
        fg2 = sb("fg2", [P, KT])
        c_act = sb("c_act", [P, KT])
        gall = sb("gall", [P, KT])
        hcol = sb("hcol", [P, 8, NHG])
        cn = sb("cn", [P, QT, NFOX])
        stat = sb("stat", [P, 6, QT])
        ssq_a = sb("ssq_a", [P, S])
        ssq_b = sb("ssq_b", [P, S])
        r1 = sb("r1", [P, S])
        wk = sb("wk", [P, 4, S])
        ones, ident, starts = consts[:, 0:P], consts[:, P:2 * P], consts[:, 2 * P:2 * P + S]
        eye_b, causal_b, chunk_b = masks[:, 0, :], masks[:, 1, :], masks[:, 2, :]

        def col(name, k=0, n=1):
            return cols[:, COLS[name][0] + k:COLS[name][0] + k + n]

        one_c, eps_c = col("one"), col("eps")

        mkv = sb("mkv", [P, 2, NMEMH, MEM])
        ada_ring = mkv[:, :, :, :].rearrange("p a h m -> p (a h m)")[:, 0:2 * ADA_COLS].rearrange("p (s n) -> p s n", s=2)
        with ExitStack() as early:
            mem_hi = sb("mem_hi", [P, KT, MEM], F32R, early)
            mem_lo = sb("mem_lo", [P, KT, MEM], F32R, early)
        first = ExitStack()
        qkv = sb("qkv", [P, 4, S], F32, first)
        tp = sb("tp", [P, 2, 1280], F32, first)
        upad = sb("upad", [P, NCONV, TAPS - 1 + S], F32, first)
        pwt = upad[:, :, 0:S]
        ctmp = sb("ctmp", [P, S], F32, first)
        ada_acc = sb("ada_acc", [P, ADA_COLS], F32, first)
        cT = sb("cT", [P, S], F32, first)
        stage1 = qkv[:, 0:2, :]
        first.close()
        second = ExitStack()
        qkv2 = sb("qkv2", [P, 4, S], F32, second)
        tp2 = sb("tp2", [P, 2, 1280], F32, second)
        bt = sb("bt", [P, 2 * P + 1], F32, second)
        second.close()
        third = ExitStack()
        hqk = sb("hqk", [P, 2, S], F32, third)
        hq, hk, stage2 = hqk[:, 0, :], hqk[:, 1, :], hqk
        hb = sb("hb", [P, S], F32, third)
        heb = sb("heb", [P, S], F32, third)
        hqd = sb("hqd", [P, S], F32, third)
        hkd = sb("hkd", [P, S], F32, third)
        hz = sb("hz", [P, 2, S], F32, third)
        hd = sb("hd", [P, 2, S], F32, third)
        hvT = sb("hvT", [P, S], F32, third)
        hvn = sb("hvn", [P, QT, P], F32, third)
        hkn = sb("hkn", [P, QT, P], F32, third)
        hA = sb("hA", [P, QT, P], F32, third)
        hS = sb("hS", [P, NCH - 1, P], F32, third)
        third.close()

        ps_p = ctx.enter_context(nc.psum_tensor("ps_p", [P, 2, S], F32))
        ps_s = ctx.enter_context(nc.psum_tensor("ps_s", [P, 2, S], F32))
        ps_t = ctx.enter_context(nc.psum_tensor("ps_t", [P, 2, S], F32))
        ps_o = ctx.enter_context(nc.psum_tensor("ps_o", [P, S], F32))
        ps_x = ctx.enter_context(nc.psum_tensor("ps_x", [P, S], F32))

        s_const = sem("s_const")
        s_mem = sem("s_mem")
        s_x = [sem(f"s_x{n}") for n in range(4)]
        s_raw = [sem("s_raw0"), sem("s_raw1")]
        s_ada = [sem("s_ada0"), sem("s_ada1")]
        s_stage = [sem("s_stage0"), sem("s_stage1")]
        s_bias = sem("s_bias")
        s_pw = sem("s_pw")
        s_store = [sem("s_store0"), sem("s_store1")]
        w_hi_done = sem("w_hi_done")
        w_split = sem("w_split")
        proj_done = sem("proj_done")
        evac = [sem("evac0"), sem("evac1")]
        mem_split = sem("mem_split")
        moving = sem("moving")
        moving_hi = sem("moving_hi")
        conv_in = sem("conv_in")
        conv_out = sem("conv_out")
        ada_used = sem("ada_used")
        sqs = sem("sqs")
        sq_x = sem("sq_x")
        heads = dict(memh=1, fox=1, att=1)
        c_qk = Count(sem("qk_ready"), **heads)
        c_sf = Count(sem("scores_full"), memh=2, fox=4, att=4, hg=NLEV)
        c_se = Count(sem("scores_free"), memh=2, fox=4, att=4, hg=NLEV)
        c_nm = Count(sem("max_ready"), memh=1, fox=4, att=4)
        c_ex = Count(sem("exp_done"), memh=1, fox=4, att=4)
        c_pr = Count(sem("probs_ready"), **heads)
        c_tf = Count(sem("probsT_full"), memh=2, fox=4, att=4)
        c_te = Count(sem("probsT_ready"), memh=2, fox=4, att=4)
        c_vt = Count(sem("value_ready"), mem_a=1, mem_b=1, memh=1, fox=1, att=1, hg=1)
        c_of = Count(sem("heads_full"), memh=1, fox=1, att=1, hg=1)
        c_oe = Count(sem("heads_done"), memh=1, fox=1, att=1, hg=1)
        gates = dict(conv=1, flog=1, memh=1, cums=1, fox=1, gate=4, att=1, hg=3)
        c_ge = Count(sem("gate_soft"), **gates)
        c_gu = Count(sem("gate_log"), **gates)
        c_gs = Count(sem("gate_sig"), **gates)
        c_xf = Count(sem("side_full"), start=1, mem_a=1, xnorm=1, mem_b=1, cums=1, fox=3, gate=2, norm2=1,
                     att=3, hg=3)
        c_xe = Count(sem("side_free"), start=1, mem_a=1, xnorm=1, mem_b=1, cums=1, fox=3, gate=2, norm2=1,
                     att=3, hg=3)
        c_in = Count(sem("side_in"), xnorm=1, cums=1, fox=2, gate=2, norm2=1, att=2, hg=1)
        c_ln = Count(sem("ln_ready"), gate=4)
        c_le = Count(sem("ln_soft"), gate=4)
        c_lu = Count(sem("ln_log"), gate=4)
        c_ls = Count(sem("ln_sig"), gate=4)
        lb_exp = sem("lb_exp")
        c_uc = Count(sem("pw_in"), gate=1)
        c_pf = Count(sem("pw_full"), pw=4)
        c_yc = Count(sem("pw_done"), pw=4)
        c_sq = Count(sem("squares"), out1=2)
        c_tt = Count(sem("residual"), out1=2)
        c_u2 = Count(sem("norm2_tiles"), norm2=16)
        c_r2 = Count(sem("norm2_rows"), norm2=3)
        c_m2 = Count(sem("norm2_mean"), norm2=1)
        c_sg = Count(sem("norm_sq"), att=2)
        c_rr = Count(sem("norm_rows"), att=2, hg=1)
        c_bt = Count(sem("bias_used"), att=1)
        c_lf = Count(sem("forget_log"), hg=1)
        c_b = Count(sem("decay_ready"), hg=1)
        c_eb = Count(sem("decay_exp"), hg=1)
        c_dd = Count(sem("level_diff"), hg=7)
        c_de = Count(sem("level_exp"), hg=7)
        c_qr = Count(sem("query_ready"), hg=1)
        c_dz = Count(sem("level_in"), hg=7)
        c_qd = Count(sem("query_decayed"), hg=1)
        c_A = Count(sem("scores_masked"), hg=1)
        c_kvf = Count(sem("kv_full"), hg=2)
        c_st = Count(sem("states_ready"), hg=1)
        c_so = Count(sem("heads_sq"), hg=1)
        s_out = sem("s_out")
        credited = [w_hi_done, w_split, proj_done, *evac, moving, moving_hi] + [
            c.sem for c in (c_qk, c_sf, c_se, c_nm, c_ex, c_pr, c_tf, c_te, c_vt, c_of, c_oe, c_ge, c_xf, c_xe,
                            c_in, c_ln, c_le, c_lu, c_ls, c_gu, c_gs, c_uc, c_pf, c_yc, c_sq, c_tt, c_u2, c_r2, c_m2, c_sg, c_rr, c_bt,
                            c_lf, c_b, c_eb, c_dd, c_de, c_qr, c_dz, c_qd, c_A, c_kvf, c_st,
                            c_so)]
        own = {n: sem(f"own_{n}") for n in ("act", "dve", "pool")}

        CAUSAL = [128 * i * (i + 1) // 2 for i in range(QT)]
        CAUSAL_T = [0, 512, 896, 1152]

        def tile_no(phase, i, j):
            return PHASES[phase][1] * i + (TILE0[phase] + j)

        def half(phase, i, j):
            return PHASES[phase][1] // 2 * i + (TILE0[phase] + j) // 2

        def slot(phase, j):
            return (TILE0[phase] + j) % 2

        def loop(eng, phase, body, peel=0, order=None):
            n = PHASES[phase][0]

            def once(i):
                if order is not None:
                    order.again()
                body(i)
                if order is not None:
                    order.settle()

            if order is not None:
                order.settle()
            if n - peel > 1:
                with eng.Fori(0, n - peel) as i:
                    once(i)
            else:
                peel = n
            for i in range(n - peel, n):
                once(i)

        block = ctx.enter_context(nc.Block())

        @block.sync
        def _(sp):
            for c in credited:
                sp.sem_inc(c, 1)
            sp.dma_start(Y[:, 0:8, :].rearrange("p k s -> p (k s)"), memT).then_inc(s_mem, 16)
            sp.dma_start(raw[:, 0, :], wt[0]).then_inc(s_raw[0], 16)
            sp.dma_start(cols[:, :], cols_d).then_inc(s_const, 16)
            sp.dma_start(consts[:, :], consts_d).then_inc(s_const, 16)
            sp.dma_start(masks[:, :, :], masks_d).then_inc(s_const, 16)
            sp.dma_start(raw[:, 1, :], wt[1]).then_inc(s_raw[1], 16)
            for g in (2, 3):
                sp.dma_start(Y[:, 4 * g:4 * g + 4, :], xT[:, 4 * g:4 * g + 4, :]).then_inc(s_x[g], 16)

            def load(phase, i, j, ahead=3):
                t = tile_no(phase, i, j)
                if isinstance(t, int) and t + ahead >= NTILES:
                    return
                sp.wait_ge(w_split, t + ahead)
                s = (TILE0[phase] + j + ahead) % 2
                sp.dma_start(raw[:, s, :], wt[t + ahead]).then_inc(s_raw[s], 16)

            load("start", 0, 0, 2)
            sp.wait_ge(mem_split, KT)
            for g in (0, 1):
                sp.dma_start(Y[:, 4 * g:4 * g + 4, :], xT[:, 4 * g:4 * g + 4, :]).then_inc(s_x[g], 16)
            for phase in ("mem_a", "mem_b", "conv"):
                loop(sp, phase, lambda i: [load(phase, i, j) for j in range(2)])
            load("flog", 0, 0)
            loop(sp, "memh", lambda i: [load("memh", i, j) for j in range(2)])
            sp.wait_ge(c_vt.sem, c_vt.at("memh", 3, 1))
            sp.wait_ge(c_sf.sem, c_sf.at("memh", 3, 2))

            def fox(i):
                n = 0
                for j in range(4):
                    load("fox", i, j)
                    for _ in range((4, 6, 0, 6)[j]):
                        sp.wait_ge(ada_used, 16 * i + max(n - 1, 0) + (1 if n else 1))
                        sp.dma_start(ada_ring[:, n % 2, :], ada[i, n]).then_inc(s_ada[n % 2], 16)
                        n += 1

            loop(sp, "fox", fox)
            for j in range(4):
                load("gate", 0, j)
            sp.wait_ge(conv_out, 1)
            sp.dma_start(pwt, pw).then_inc(s_pw, 16)

            sp.wait_ge(c_pf.sem, c_pf.at("pw", 0, 4))
            for j in range(2):
                sp.dma_start(stage1[:, j, :], xT[:, j, :]).then_inc(s_stage[j], 16)

            def out1(i):
                for j in range(2):
                    load("out1", i, j)
                    sp.wait_ge(c_tt.sem, c_tt.at("out1", i, j + 1))
                    sp.dma_start(spill[2 * i + j], Y[:, 2 * i + j, :]).then_inc(s_store[j], 16)
                    if not (isinstance(i, int) and i == 7):
                        sp.dma_start(stage1[:, j, :], xT[:, 2 * i + (2 + j), :]).then_inc(s_stage[j], 16)

            loop(sp, "out1", out1, peel=1)

            def att(i):
                sp.wait_ge(c_bt.sem, c_bt.at("att", i, 0))
                sp.dma_start(bt[:, :], bias[i]).then_inc(s_bias, 16)
                for j in range(4):
                    load("att", i, j)

            sp.wait_ge(c_u2.sem, c_u2.at("norm2", 0, 1))
            loop(sp, "att", att)
            loop(sp, "hg", lambda i: [load("hg", i, j) for j in range(4)])
            for j in range(2):
                sp.wait_ge(s_store[j], 16 * 8)
            for j in range(2):
                sp.dma_start(stage2[:, j, :], spill[j]).then_inc(s_stage[j], 16)

            def out2(i):
                for j in range(2):
                    load("out2", i, j)
                    sp.wait_ge(s_out, 2 * i + j + 1)
                    sp.dma_start(out[2 * i + j], wk[:, j, :]).then_inc(s_store[j], 16)
                    if not (isinstance(i, int) and i == 7):
                        sp.dma_start(stage2[:, j, :], spill[2 * i + (2 + j)]).then_inc(s_stage[j], 16)

            loop(sp, "out2", out2, peel=2)
            for j in range(2):
                sp.wait_ge(s_store[j], 16 * 16)

        @block.tensor
        def _(pe):
            mm = pe.matmul

            def project(phase, i, j, hi=act_hi, lo=act_lo, n=S, order=range(KT), hooks=None, use=None):
                s = slot(phase, j)
                pe.wait_ge(w_split, tile_no(phase, i, j) + 2)
                pe.wait_ge(evac[s], half(phase, i, j) + 1)
                for at, k in enumerate(order):
                    if use is not None:
                        pe.wait_ge(moving, 1 + KT * use + at + 1)
                    wh, wl = w_hi[:, s, k * P:(k + 1) * P], w_lo[:, s, k * P:(k + 1) * P]
                    o = ps_p[:, s, 0:n]
                    mm(o, wh, hi[:, k, 0:n], start=at == 0, stop=False)
                    mm(o, wh, lo[:, k, 0:n], start=False, stop=False)
                    last = mm(o, wl, hi[:, k, 0:n], start=False, stop=at == KT - 1)
                    if at == KT - 1:
                        last.then_inc(proj_done, 1)
                    if hooks and at in hooks:
                        hooks[at]()

            def side(phase, i, k, body):
                pe.wait_ge(c_xe.sem, c_xe.at(phase, i, k))
                body().then_inc(c_xf.sem, 1)

            def turn_value(phase, i, k, src, n):
                def body():
                    pe.wait_ge(c_vt.sem, c_vt.at(phase, i, 1))
                    for t in range(n):
                        last = pe.transpose(ps_x[:, t * P:(t + 1) * P], src[:, t * P:(t + 1) * P], ident)
                    return last
                side(phase, i, k, body)

            pe.wait_ge(s_const, 48)

            def mem_ssq():
                for k in range(KT):
                    pe.wait_ge(sqs, k + 1)
                    last = mm(ps_x[:, 0:MEM], ones, wk[:, k % 4, 0:MEM], start=k == 0, stop=k == KT - 1)
                    last_k = last
                    if k < KT - 1:
                        last.then_inc(sq_x, 1)
                return last_k
            side("start", 0, 0, mem_ssq)

            def mem(phase):
                def body(i):
                    project(phase, i, 0, mem_hi, mem_lo, MEM)
                    project(phase, i, 1, mem_hi, mem_lo, MEM,
                            hooks={8: lambda: turn_value(phase, i, 0, wk[:, 3, :], MT)})
                return body

            pe.wait_ge(mem_split, 16)
            loop(pe, "mem_a", mem("mem_a"))

            def sum_rows(src, phase, i, k):
                def body():
                    pe.wait_ge(c_in.sem, c_in.at(phase, i, k + 1))
                    return mm(ps_x[:, :], ones, src, start=True, stop=True)
                return body
            side("xnorm", 0, 0, sum_rows(ssq_a[:, :], "xnorm", 0, 0))
            loop(pe, "mem_b", mem("mem_b"))
            pe.wait_ge(moving, 1 + KT)
            loop(pe, "conv", lambda i: [project("conv", i, j) for j in range(2)])
            project("flog", 0, 0)

            def scores(phase, i, t, q, k, mask):
                pe.wait_ge(c_qk.sem, c_qk.at(phase, i, 1))
                pe.wait_ge(c_se.sem, c_se.at(phase, i, max(t - 1, 0)))
                w = P * (t + 1)
                mm(ps_s[:, t % 2, 0:w], q[:, t * P:(t + 1) * P], k[:, 0:w], start=True, stop=False,
                   skip_group_check=True)
                mm(ps_s[:, t % 2, w - P:w], eye_b, mask, start=False, stop=True,
                   skip_group_check=True).then_inc(c_sf.sem, 1)

            def turn_probs(phase, i, j, pr):
                pe.wait_ge(c_pr.sem, c_pr.at(phase, i, 1))
                pe.wait_ge(c_te.sem, c_te.at(phase, i, max(j - 1, 0)))
                for t in range(j, QT):
                    last = pe.transpose(ps_t[:, j % 2, (t - j) * P:(t - j + 1) * P],
                                        pr[:, CAUSAL[t] + j * P:CAUSAL[t] + (j + 1) * P], ident)
                last.then_inc(c_tf.sem, 1)

            def weigh(phase, i, k, v, pt):
                pe.wait_ge(c_oe.sem, c_oe.at(phase, i, 0))
                pe.wait_ge(c_xe.sem, c_xe.at(phase, i, k))
                for j in range(QT):
                    pe.wait_ge(c_te.sem, c_te.at(phase, i, j + 1))
                    last = mm(ps_o[:, j * P:S], v[:, j * P:(j + 1) * P], pt[:, CAUSAL_T[j]:CAUSAL_T[j] + S - j * P],
                              start=j == 0, stop=j == QT - 1, skip_group_check=True)
                last.then_inc(c_of.sem, 1)

            def memh(i):
                def s2(b):
                    pe.wait_ge(c_qk.sem, c_qk.at("memh", i, 1))
                    pe.wait_ge(c_se.sem, c_se.at("memh", i, 0))
                    for t in (2 * b, 2 * b + 1):
                        last = mm(ps_s[:, b, (t % 2) * MEM:(t % 2 + 1) * MEM], qkv[:, 0, t * P:(t + 1) * P],
                                  mkv[:, 0, i, :], start=True, stop=True, skip_group_check=True)
                    last.then_inc(c_sf.sem, 1)

                def t2(j):
                    pe.wait_ge(c_pr.sem, c_pr.at("memh", i, 1))
                    pe.wait_ge(c_te.sem, c_te.at("memh", i, 0))
                    for t in range(QT):
                        last = pe.transpose(ps_t[:, j, t * P:(t + 1) * P],
                                            tp[:, 0, t * MEM + j * P:t * MEM + (j + 1) * P], ident)
                    last.then_inc(c_tf.sem, 1)

                project("memh", i, 0)
                project("memh", i, 1, hooks={3: lambda: s2(0), 4: lambda: s2(1), 12: lambda: t2(0),
                                             13: lambda: t2(1)})
                pe.wait_ge(c_oe.sem, c_oe.at("memh", i, 0))
                pe.wait_ge(c_vt.sem, c_vt.at("memh", i, 1))
                for j in range(MT):
                    pe.wait_ge(c_te.sem, c_te.at("memh", i, j + 1))
                    last = mm(ps_o[:, :], qkv[:, 3, j * P:(j + 1) * P], tp[:, 1, j * S:(j + 1) * S],
                              start=j == 0, stop=j == MT - 1)
                last.then_inc(c_of.sem, 1)
            loop(pe, "memh", memh)

            def c_columns():
                pe.wait_ge(c_in.sem, c_in.at("cums", 0, 1))
                for t in range(QT):
                    last = pe.transpose(ps_x[:, t * NFOX:(t + 1) * NFOX], cT[0:NFOX, t * P:(t + 1) * P],
                                        ident[0:NFOX, 0:NFOX])
                return last
            side("cums", 0, 0, c_columns)

            def fox(i):
                def spread_c():
                    pe.wait_ge(c_in.sem, c_in.at("fox", i, 1))
                    return mm(ps_x[:, :], ones[0:NFOX, :], wk[0:NFOX, 0, :], start=True, stop=True)

                def ada_sum():
                    pe.wait_ge(c_in.sem, c_in.at("fox", i, 2))
                    for m in range(6):
                        last = mm(ps_x[:, m:m + 1], ada_acc[:, m * P:(m + 1) * P], one_c, start=True, stop=True)
                    return last

                q, k, v = qkv[:, 0, :], qkv[:, 1, :], qkv[:, 2, :]
                project("fox", i, 0, hooks={3: lambda: side("fox", i, 0, spread_c)})
                project("fox", i, 1)
                project("fox", i, 2, hooks={4: lambda: scores("fox", i, 0, q, k, causal_b),
                                            5: lambda: scores("fox", i, 1, q, k, causal_b),
                                            9: lambda: scores("fox", i, 2, q, k, causal_b),
                                            12: lambda: scores("fox", i, 3, q, k, causal_b)})
                project("fox", i, 3, hooks={4: lambda: turn_value("fox", i, 1, v, QT),
                                            8: lambda: turn_probs("fox", i, 0, tp[:, 0, :]),
                                            9: lambda: turn_probs("fox", i, 1, tp[:, 0, :]),
                                            11: lambda: turn_probs("fox", i, 2, tp[:, 0, :]),
                                            12: lambda: turn_probs("fox", i, 3, tp[:, 0, :])})
                weigh("fox", i, 2, qkv[:, 3, :], tp[:, 1, :])
                side("fox", i, 2, ada_sum)
            loop(pe, "fox", fox)

            def channel_sum(k):
                def body():
                    pe.wait_ge(c_in.sem, c_in.at("gate", 0, k + 1))
                    for c in range(NCONV):
                        last = mm(ps_x[:, :], ones, (Y[:, c, :], qkv[:, c, :])[k], start=c == 0, stop=c == NCONV - 1)
                    return last
                return lambda: side("gate", 0, k, body)
            project("gate", 0, 0, hooks={3: channel_sum(0)})
            project("gate", 0, 1, hooks={3: channel_sum(1)})
            project("gate", 0, 2)
            project("gate", 0, 3)
            pe.wait_ge(s_pw, 16)
            pe.wait_ge(c_uc.sem, c_uc.at("gate", 0, 1))
            for m in range(NCONV):
                bank = (ps_s[:, 0, :], ps_s[:, 1, :], ps_t[:, 0, :], ps_t[:, 1, :])[m]
                for c in range(NCONV):
                    last = mm(bank, pwt[:, c, m * P:(m + 1) * P], qkv[:, c, :], start=c == 0, stop=c == NCONV - 1)
                last.then_inc(c_pf.sem, 1)

            late = [*range(4, KT), *range(4)]
            loop(pe, "out1", lambda i: [project("out1", i, j, order=late, use=1) for j in range(2)])

            def both_sums():
                pe.wait_ge(c_in.sem, c_in.at("norm2", 0, 1))
                mm(ps_o[:, :], ones, ssq_b[:, :], start=True, stop=True)
                return mm(ps_x[:, :], ones, ssq_a[:, :], start=True, stop=True)
            side("norm2", 0, 0, both_sums)

            def att(i):
                q, k, v = qkv2[:, 0, :], qkv2[:, 1, :], qkv2[:, 2, :]
                project("att", i, 0, use=2)
                project("att", i, 1, hooks={3: lambda: side("att", i, 0, sum_rows(wk[:, 0, :], "att", i, 0))})
                project("att", i, 2, hooks={3: lambda: side("att", i, 1, sum_rows(wk[:, 0, :], "att", i, 1)),
                                            10: lambda: scores("att", i, 0, q, k, chunk_b),
                                            11: lambda: scores("att", i, 1, q, k, chunk_b),
                                            14: lambda: scores("att", i, 2, q, k, chunk_b)})
                project("att", i, 3, hooks={1: lambda: scores("att", i, 3, q, k, chunk_b),
                                            4: lambda: turn_value("att", i, 2, v, QT),
                                            11: lambda: turn_probs("att", i, 0, tp2[:, 0, :]),
                                            12: lambda: turn_probs("att", i, 1, tp2[:, 0, :]),
                                            13: lambda: turn_probs("att", i, 2, tp2[:, 0, :]),
                                            14: lambda: turn_probs("att", i, 3, tp2[:, 0, :])})
                weigh("att", i, 3, qkv2[:, 3, :], tp2[:, 1, :])
            loop(pe, "att", att)

            def hg(i):
                def level(n):
                    def body():
                        pe.wait_ge(c_se.sem, c_se.at("hg", i, max(n - 1, 0)))
                        if n:
                            pe.wait_ge(c_dz.sem, c_dz.at("hg", i, n + 1))
                            left = right = hz[:, (n - 1) % 2, :]
                        else:
                            pe.wait_ge(c_qr.sem, c_qr.at("hg", i, 1))
                            left, right = hk, hq
                        for t in range(QT):
                            last = mm(ps_s[:, n % 2, t * P:(t + 1) * P], left[:, t * P:(t + 1) * P],
                                      right[:, t * P:(t + 1) * P], start=True, stop=True, skip_group_check=True)
                        last.then_inc(c_sf.sem, 1)
                    return body

                def turn_keys():
                    pe.wait_ge(c_dz.sem, c_dz.at("hg", i, 1))
                    for t in range(QT):
                        last = pe.transpose(ps_x[:, t * P:(t + 1) * P], hkd[:, t * P:(t + 1) * P], ident)
                    return last

                def chunk_states():
                    pe.wait_ge(c_xe.sem, c_xe.at("hg", i, 2))
                    pe.wait_ge(c_st.sem, c_st.at("hg", i, 0))
                    for n in (0, 2, 4, 6, 1, 3, 5):
                        rows = slice(n % 2 * CHUNK, n % 2 * CHUNK + CHUNK)
                        last = mm(ps_t[:, n % 2, n // 2 * P:(n // 2 + 1) * P], hkn[rows, n // 2, :],
                                  hvn[rows, n // 2, :], start=True, stop=True, skip_group_check=True)
                        if n in (6, 5):
                            last.then_inc(c_kvf.sem, 1)

                def within():
                    pe.wait_ge(c_oe.sem, c_oe.at("hg", i, 0))
                    pe.wait_ge(c_A.sem, c_A.at("hg", i, 1))
                    for t in range(QT):
                        mm(ps_o[:, t * P:(t + 1) * P], hvn[:, t, :], hA[:, t, :], start=t == 0, stop=False,
                           skip_group_check=True)

                def across():
                    pe.wait_ge(c_qd.sem, c_qd.at("hg", i, 1))
                    pe.wait_ge(c_st.sem, c_st.at("hg", i, 1))
                    for n in range(1, NCH):
                        c = slice(n * CHUNK, (n + 1) * CHUNK)
                        last = mm(ps_o[:, c], hS[:, n - 1, :], hqd[:, c], start=False, stop=n == NCH - 1,
                                  skip_group_check=True)
                    last.then_inc(c_of.sem, 1)

                project("hg", i, 0)
                project("hg", i, 1, hooks={15: lambda: side("hg", i, 0, turn_keys)})
                project("hg", i, 2, hooks={3: level(0), 5: level(1), 7: level(2), 9: level(3), 11: level(4),
                                           13: level(5), 15: level(6)})
                project("hg", i, 3, hooks={3: lambda: turn_value("hg", i, 1, hvT[:, :], QT), 6: chunk_states,
                                           7: within, 11: across})
                side("hg", i, 2, sum_rows(wk[:, 0, :], "hg", i, 0))
            loop(pe, "hg", hg)
            loop(pe, "out2", lambda i: [project("out2", i, j, use=3) for j in range(2)])

        @block.scalar
        def _(act):
            o = Order(act, own["act"])
            fn = act.activation
            act.preload_act_table_set("natural_log_exp_and_others")

            def split(phase, i, j, ahead=1):
                t = tile_no(phase, i, j) + ahead
                if isinstance(t, int) and t >= NTILES:
                    return
                s = (TILE0[phase] + j + ahead) % 2
                act.wait_ge(s_raw[s], 16 * (half(phase, i, j + ahead) + 1))
                act.wait_ge(proj_done, t if not isinstance(t, int) else max(t, 1))
                fn(w_hi[:, s, :], raw[:, s, :], ACT.Copy).then_inc(w_hi_done, 1)

            def rows(dst, src, width, tmp):
                o.step(fn(tmp, src, ACT.Ln, scale=1.0 / width, bias=eps_c))
                o.settle()
                return fn(dst, tmp, ACT.Exp, scale=-0.5)

            def softplus(dst, src, bias=None):
                if bias is None:
                    o.step(fn(dst, src, ACT.Abs))
                else:
                    o.step(fn(dst, src, ACT.Abs, bias=bias))
                o.settle()
                o.step(fn(dst, dst, ACT.Exp, scale=-1.0))
                o.settle()
                return fn(dst, dst, ACT.Ln, bias=one_c[0:dst.shape[0], :])

            def sigmoid(phase, i, j, k, dst):
                act.wait_ge(proj_done, tile_no(phase, i, j) + 2)
                softplus(dst, ps_p[:, slot(phase, j), :]).then_inc(c_ge.sem, 1)
                act.wait_ge(c_gu.sem, c_gu.at(phase, i, k))
                fn(dst, dst, ACT.Exp).then_inc(c_gs.sem, 1)

            act.wait_ge(s_const, 48)
            act.wait_ge(s_mem, 16)
            memv = Y[:, 0:8, :].rearrange("p k s -> p (k s)").rearrange("p (k m) -> p k m", k=KT)
            for k in range(KT):
                if k >= 4:
                    act.wait_ge(sq_x, k - 3)
                fn(wk[:, k % 4, 0:MEM], memv[:, k, :], ACT.Square).then_inc(sqs, 1)
            split("start", 0, 0, 0)
            act.wait_ge(c_xf.sem, c_xf.at("start", 0, 1))
            rows(r1[:, 0:MEM], ps_x[:, 0:MEM], D, wk[:, 0, 0:MEM]).then_inc(c_xe.sem, 1)
            for k in range(KT):
                act.wait_ge(moving_hi, 2 + k)
                fn(mem_hi[:, k, :], wk[:, 1 + k % 2, 0:MEM], ACT.Copy).then_inc(sqs, 1)

            def x_squares(g):
                if g == 2:
                    act.wait_ge(mem_split, KT)
                for k in range(4 * g, 4 * g + 4):
                    if k % 4 == 0:
                        act.wait_ge(s_x[k // 4], 16)
                    n = (g - 2) % 4 * 4 + k % 4
                    if n >= 2:
                        act.wait_ge(sq_x, KT - 1 + n - 1)
                    fn(wk[:, n % 2, :], Y[:, k, :], ACT.Square).then_inc(sqs, 1)

            def x_hi(g):
                for k in range(4 * g, 4 * g + 4):
                    act.wait_ge(moving_hi, 2 + KT + k)
                    fn(act_hi[:, k, :], wk[:, k % 2, :], ACT.Copy).then_inc(sqs, 1)

            def mem_tile(phase, i, j, n, extra):
                split(phase, i, j)
                extra()
                if j == 0:
                    act.wait_ge(proj_done, tile_no(phase, i, j) + 2)
                    fn(wk[:, 3, 0:MEM], ps_p[:, slot(phase, j), 0:MEM], ACT.Copy).then_inc(c_vt.sem, 1)
                else:
                    act.wait_ge(c_xf.sem, c_xf.at(phase, i, 1))
                    h = (0 if phase == "mem_a" else 2) + i
                    fn(mkv[:, 1, h, :], ps_x[:, 0:MEM], ACT.Copy).then_inc(c_xe.sem, 1)

            mem_tile("mem_a", 0, 0, 0, lambda: x_squares(2))
            mem_tile("mem_a", 0, 1, 1, lambda: x_squares(3))
            mem_tile("mem_a", 1, 0, 2, lambda: x_squares(0))
            mem_tile("mem_a", 1, 1, 3, lambda: x_squares(1))
            act.wait_ge(c_xf.sem, c_xf.at("xnorm", 0, 1))
            rows(r1[:, :], ps_x[:, :], D, ssq_b[:, :]).then_inc(c_xe.sem, 1)
            for n, (i, j) in enumerate(((0, 0), (0, 1), (1, 0), (1, 1))):
                mem_tile("mem_b", i, j, n, lambda: x_hi(n))

            def conv(i):
                split("conv", i, 0)
                act.wait_ge(evac[slot("conv", 1)], half("conv", i, 1) + 1)
                sigmoid("conv", i, 0, 1, wk[:, 0, :])
                split("conv", i, 1)
            loop(act, "conv", conv, order=o)

            o.settle()
            o.again()
            split("flog", 0, 0)
            act.wait_ge(evac[slot("conv", 1)], half("conv", 3, 1) + 2)
            act.wait_ge(proj_done, tile_no("flog", 0, 0) + 2)
            f8 = ps_p[0:NFOX, slot("flog", 0), :]
            b_f = cols[0:NFOX, COLS["b_f"][0]:COLS["b_f"][0] + 1]
            o.step(fn(wk[0:NFOX, 1, :], f8, ACT.Identity, bias=b_f))
            o.settle()
            softplus(wk[0:NFOX, 1, :], wk[0:NFOX, 1, :]).then_inc(c_ge.sem, 1)
            act.sem_inc(c_gs.sem, 1)
            act.wait_ge(conv_in, 1)
            fn(hcol[:, 3:5, :], hcol[:, 3:5, :], ACT.Exp).then_inc(lb_exp, 1)

            def gate_exp(phase, i, j, k=1, dst=0):
                act.wait_ge(c_oe.sem, c_oe.at(phase, i, 0))
                sigmoid(phase, i, j, k, wk[:, dst, :])

            def memh(i):
                split("memh", i, 0)
                split("memh", i, 1)
                act.wait_ge(c_of.sem, c_of.at("memh", i, 0))
                fn(qkv[:, 3, 0:MEM], mkv[:, 1, i, :], ACT.Copy).then_inc(c_vt.sem, 1)
                act.wait_ge(c_nm.sem, c_nm.at("memh", i, 1))
                for t in range(QT):
                    e = fn(tp[:, 0, t * MEM:(t + 1) * MEM], ps_s[:, t // 2, t % 2 * MEM:(t % 2 + 1) * MEM], ACT.Exp,
                           bias=stat[:, 1, t:t + 1], accum_out=stat[:, 2, t:t + 1])
                    if t % 2:
                        e.then_inc(c_se.sem, 1)
                    else:
                        o.step(e)
                fn(stat[:, 4, 0:1], one_c, ACT.Copy).then_inc(c_ex.sem, 1)
                for j in range(MT):
                    act.wait_ge(c_tf.sem, c_tf.at("memh", i, j + 1))
                    fn(tp[:, 1, j * S:(j + 1) * S], ps_t[:, j, :], ACT.Copy).then_inc(c_te.sem, 1)
                gate_exp("memh", i, 1)
            loop(act, "memh", memh, order=o)
            o.settle()
            o.again()
            act.wait_ge(c_xf.sem, c_xf.at("cums", 0, 1))
            fn(cn[:, :, :].rearrange("p t h -> p (t h)"), ps_x[:, 0:QT * NFOX], ACT.Copy).then_inc(c_xe.sem, 1)
            softplus(c_act[:, :], col("c_2", 0, KT)).then_inc(c_ge.sem, 1)
            act.wait_ge(c_gu.sem, c_gu.at("cums", 0, 1))
            fn(c_act[:, :], c_act[:, :], ACT.Exp).then_inc(c_gs.sem, 1)

            def exps(phase, i, t, pr):
                act.wait_ge(c_nm.sem, c_nm.at(phase, i, t + 1))
                e = pr[:, CAUSAL[t]:CAUSAL[t] + P * (t + 1)]
                fn(e, e, ACT.Exp, bias=stat[:, 1, t:t + 1], accum_out=stat[:, 2, t:t + 1]).then_inc(c_ex.sem, 1)

            def probsT(phase, i, j, pt):
                act.wait_ge(c_tf.sem, c_tf.at(phase, i, j + 1))
                n = S - j * P
                fn(pt[:, CAUSAL_T[j]:CAUSAL_T[j] + n], ps_t[:, j % 2, 0:n], ACT.Copy).then_inc(c_te.sem, 1)

            def value_out(phase, i, j, dst):
                act.wait_ge(proj_done, tile_no(phase, i, j) + 2)
                o.step(fn(dst, ps_p[:, slot(phase, j), :], ACT.Copy))
                o.settle()
                act.sem_inc(evac[slot(phase, j)], 1)
                act.sem_inc(c_vt.sem, 1)

            def value_turned(phase, i, k, dst):
                act.wait_ge(c_xf.sem, c_xf.at(phase, i, k))
                fn(dst, ps_x[:, :], ACT.Copy).then_inc(c_xe.sem, 1)

            def fox(i):
                split("fox", i, 0)
                act.wait_ge(c_xf.sem, c_xf.at("fox", i, 1))
                fn(wk[:, 1, :], ps_x[:, :], ACT.Copy, scale=-1.0).then_inc(c_xe.sem, 1)
                split("fox", i, 1)
                split("fox", i, 2)
                for t in range(QT):
                    exps("fox", i, t, tp[:, 0, :])
                value_out("fox", i, 2, qkv[:, 2, :])
                split("fox", i, 3)
                value_turned("fox", i, 2, qkv[:, 3, :])
                for j in range(QT):
                    probsT("fox", i, j, tp[:, 1, :])
                gate_exp("fox", i, 3, dst=2)
            loop(act, "fox", fox, order=o)

            o.settle()
            o.again()

            def conv_gate(j):
                if j:
                    act.wait_ge(evac[slot("gate", j - 1)], half("gate", 0, j - 1) + 2)
                sigmoid("gate", 0, j, j + 1, wk[:, 2, :])

            split("gate", 0, 0)
            act.wait_ge(c_ln.sem, c_ln.at("gate", 0, 1))
            for c in range(NCONV):
                e = fn(qkv[:, c, :], Y[:, c, :], ACT.Square)
                if c < NCONV - 1:
                    o.step(e)
                else:
                    e.then_inc(c_in.sem, 1)
            conv_gate(0)
            split("gate", 0, 1)
            act.wait_ge(c_xf.sem, c_xf.at("gate", 0, 2))
            rows(r1[:, :], ps_x[:, :], NCONV * P, ssq_b[:, :]).then_inc(c_xe.sem, 1)
            conv_gate(1)
            split("gate", 0, 2)
            act.wait_ge(c_ln.sem, c_ln.at("gate", 0, 2))
            for c in range(NCONV):
                o.step(fn(Y[:, c, :], Y[:, c, :], ACT.Identity, scale=col("conv_ln_g", c), bias=col("conv_ln_b", c)))
            o.settle()
            for c in range(NCONV):
                softplus(qkv[:, c, :], Y[:, c, :]).then_inc(c_le.sem, 1)
                act.wait_ge(c_lu.sem, c_lu.at("gate", 0, c + 1))
                fn(qkv[:, c, :], qkv[:, c, :], ACT.Exp).then_inc(c_ls.sem, 1)
            conv_gate(2)
            split("gate", 0, 3)
            conv_gate(3)

            def y_hi(order_, use):
                for k in order_:
                    fn(act_hi[:, k, :], Y[:, k, :], ACT.Copy).then_inc(moving_hi, 1)

            act.wait_ge(proj_done, tile_no("out1", 0, 0) + 1)
            act.wait_ge(c_oe.sem, c_oe.at("fox", 7, 1))
            y_hi(range(4, KT), 1)
            for m in range(NCONV):
                act.wait_ge(c_yc.sem, c_yc.at("pw", 0, m + 1))
                y_hi([m], 1)

            def out1(i):
                for j in range(2):
                    split("out1", i, j)
                    act.wait_ge(c_tt.sem, c_tt.at("out1", i, j + 1))
                    fn(wk[:, j, :], Y[:, 2 * i + j, :], ACT.Square).then_inc(c_sq.sem, 1)
            loop(act, "out1", out1, order=o)
            o.settle()
            o.again()
            act.wait_ge(c_xf.sem, c_xf.at("norm2", 0, 1))
            rows(r1[:, :], ps_x[:, :], D, wk[:, 2, :]).then_inc(c_r2.sem, 1)
            act.wait_ge(c_m2.sem, c_m2.at("norm2", 0, 1))
            rows(wk[:, 2, :], wk[:, 3, :], D, wk[:, 2, :]).then_inc(c_r2.sem, 1)
            for k in range(KT):
                act.wait_ge(c_u2.sem, c_u2.at("norm2", 0, k + 1))
                fn(act_hi[:, k, :], wk[:, k % 2, :], ACT.Identity, bias=mod[:, k:k + 1]).then_inc(moving_hi, 1)

            def att(i):
                def norm(j, n):
                    act.wait_ge(proj_done, tile_no("att", i, j) + 2)
                    if j == 0:
                        act.wait_ge(c_oe.sem, c_oe.at("att", i, 0))
                    fn(wk[:, 0, :], ps_p[:, slot("att", j), :], ACT.Square).then_inc(c_in.sem, 1)

                def norm_rows(j):
                    act.wait_ge(c_xf.sem, c_xf.at("att", i, j + 1))
                    o.step(fn(wk[:, 1, :], ps_x[:, :], ACT.Ln, scale=1.0 / P, bias=eps_c))
                    o.settle()
                    act.sem_inc(c_xe.sem, 1)
                    fn(wk[:, 1, :], wk[:, 1, :], ACT.Exp, scale=-0.5).then_inc(c_rr.sem, 1)

                split("att", i, 0)
                norm(0, 0)
                split("att", i, 1)
                norm_rows(0)
                norm(1, 1)
                split("att", i, 2)
                norm_rows(1)
                for t in range(3):
                    exps("att", i, t, tp2[:, 0, :])
                value_out("att", i, 2, qkv2[:, 2, :])
                split("att", i, 3)
                exps("att", i, 3, tp2[:, 0, :])
                value_turned("att", i, 3, qkv2[:, 3, :])
                for j in range(QT):
                    probsT("att", i, j, tp2[:, 1, :])
                gate_exp("att", i, 3, dst=2)
            loop(act, "att", att, order=o)

            def hg(i):
                split("hg", i, 0)
                act.wait_ge(proj_done, tile_no("hg", i, 0) + 2)
                softplus(wk[:, 1, :], ps_p[:, slot("hg", 0), :]).then_inc(c_ge.sem, 1)
                split("hg", i, 1)
                act.wait_ge(c_gu.sem, c_gu.at("hg", i, 1))
                act.wait_ge(c_dz.sem, c_dz.at("hg", i, 0))
                act.wait_ge(c_sf.sem, c_sf.at("hg", i, 0))
                o.step(fn(wk[:, 0, :], wk[:, 0, :], ACT.Exp))
                fn(hk, wk[:, 1, :], ACT.Exp, scale=-1.0).then_inc(c_gs.sem, 1)
                o.settle()
                fn(hd[:, 0, :], wk[:, 0, :], ACT.Ln, scale=hcol[:, 1, bass.ds(i, 1)],
                   bias=hcol[:, 2, bass.ds(i, 1)]).then_inc(c_lf.sem, 1)
                act.wait_ge(c_b.sem, c_b.at("hg", i, 1))
                fn(heb[:, :], hb[:, :], ACT.Exp).then_inc(c_eb.sem, 1)

                def level_exp(n):
                    act.wait_ge(c_dd.sem, c_dd.at("hg", i, n + 1))
                    d = hd[:, n % 2, :]
                    if n:
                        o.step(fn(d, d, ACT.Abs))
                        o.settle()
                    fn(d, d, ACT.Exp, scale=-1.0).then_inc(c_de.sem, 1)
                level_exp(0)
                sigmoid("hg", i, 1, 2, wk[:, 3, :])
                split("hg", i, 2)
                act.wait_ge(c_xf.sem, c_xf.at("hg", i, 1))
                fn(hkn[:, :, :].rearrange("p t d -> p (t d)"), ps_x[:, :], ACT.Copy).then_inc(c_xe.sem, 1)
                for n in range(1, NLEV):
                    level_exp(n)
                value_out("hg", i, 2, hvT[:, :])
                split("hg", i, 3)
                value_turned("hg", i, 2, hvn[:, :, :].rearrange("p t d -> p (t d)"))
                act.wait_ge(c_of.sem, c_of.at("hg", i, 1))
                fn(wk[:, 0, :], ps_o[:, :], ACT.Square).then_inc(c_in.sem, 1)
                sigmoid("hg", i, 3, 3, wk[:, 2, :])
                act.wait_ge(c_xf.sem, c_xf.at("hg", i, 3))
                o.step(fn(ssq_a[:, :], ps_x[:, :], ACT.Ln, scale=1.0 / P, bias=eps_c))
                o.settle()
                act.sem_inc(c_xe.sem, 1)
                fn(ssq_a[:, :], ssq_a[:, :], ACT.Exp, scale=-0.5).then_inc(c_rr.sem, 1)
            loop(act, "hg", hg, order=o)
            act.wait_ge(proj_done, tile_no("out2", 0, 0) + 1)
            for k in range(KT):
                if k == KT - 1:
                    act.wait_ge(c_oe.sem, c_oe.at("hg", 7, 1))
                elif k == 0:
                    act.wait_ge(c_oe.sem, c_oe.at("hg", 7, 0))
                fn(act_hi[:, k, :], Y[:, k, :], ACT.Copy).then_inc(moving_hi, 1)

            def out2(i):
                split("out2", i, 0)
                split("out2", i, 1)
            loop(act, "out2", out2, peel=1)

        @block.vector
        def _(dve):
            o = Order(dve, own["dve"])
            tt, ts, stt = dve.tensor_tensor, dve.tensor_scalar, dve.scalar_tensor_tensor

            def do(ins):
                o.step(ins)
                o.settle()

            def split(phase, i, j, ahead=1):
                t = tile_no(phase, i, j) + ahead
                if isinstance(t, int) and t >= NTILES:
                    return
                s = (TILE0[phase] + j + ahead) % 2
                dve.wait_ge(w_hi_done, t + 2)
                tt(w_lo[:, s, :], raw[:, s, :], w_hi[:, s, :].bitcast(F32), ALU.subtract).then_inc(w_split, 1)

            def log_sigmoid(phase, i, j, k, dst):
                dve.wait_ge(c_ge.sem, c_ge.at(phase, i, k))
                stt(dst, ps_p[:, slot(phase, j), :], 0.0, dst, ALU.min, ALU.subtract).then_inc(c_gu.sem, 1)
                dve.wait_ge(c_gs.sem, c_gs.at(phase, i, k))

            memv = Y[:, 0:8, :].rearrange("p k s -> p (k s)").rearrange("p (k m) -> p k m", k=KT)
            dve.wait_ge(s_const, 48)
            dve.wait_ge(s_mem, 16)
            split("start", 0, 0, 0)
            dve.wait_ge(c_xe.sem, c_xe.at("start", 0, 1))
            for k in range(KT):
                if k >= 2:
                    dve.wait_ge(sqs, KT + k - 1)
                    dve.wait_ge(mem_split, k - 1)
                stt(wk[:, 1 + k % 2, 0:MEM], memv[:, k, :], col("mem_norm_g", k), r1[:, 0:MEM], ALU.mult,
                    ALU.mult).then_inc(moving_hi, 1)
                if k:
                    dve.wait_ge(sqs, KT + k)
                    tt(mem_lo[:, k - 1, :], wk[:, 1 + (k - 1) % 2, 0:MEM], mem_hi[:, k - 1, :].bitcast(F32),
                       ALU.subtract).then_inc(mem_split, 1)
            dve.wait_ge(sqs, 2 * KT)
            tt(mem_lo[:, KT - 1, :], wk[:, 2, 0:MEM], mem_hi[:, KT - 1, :].bitcast(F32),
               ALU.subtract).then_inc(mem_split, 1)
            dve.wait_ge(mem_split, 16)
            dve.memset(ssq_a[:, :], 0.0).then_inc(mem_split, 1)

            def x_sums(g):
                for k in range(4):
                    n = (g - 2) % 4 * 4 + k
                    dve.wait_ge(sqs, 2 * KT + n + 1)
                    dve.wait_ge(mem_split, 17) if n == 0 else dve.wait_ge(sq_x, KT - 1 + n)
                    tt(ssq_a[:, :], ssq_a[:, :], wk[:, n % 2, :], ALU.add).then_inc(
                        sq_x if n < KT - 1 else c_in.sem, 1)

            def x_norm(g):
                for k in range(4 * g, 4 * g + 4):
                    if k >= 2:
                        dve.wait_ge(moving, 1 + k - 1)
                    stt(wk[:, k % 2, :], Y[:, k, :], col("norm_g", k), r1[:, :], ALU.mult, ALU.mult).then_inc(
                        moving_hi, 1)
                    if k:
                        x_lo(k - 1)
                if g == 3:
                    x_lo(KT - 1)

            def x_lo(k):
                dve.wait_ge(sqs, 3 * KT + k + 1)
                tt(act_lo[:, k, :], wk[:, k % 2, :], act_hi[:, k, :].bitcast(F32), ALU.subtract).then_inc(moving, 1)

            def mem_tile(phase, i, j, extra):
                split(phase, i, j)
                extra()
                s = slot(phase, j)
                if j == 0:
                    dve.wait_ge(c_vt.sem, c_vt.at(phase, i, 1))
                    dve.sem_inc(evac[s], 1)
                else:
                    dve.wait_ge(proj_done, tile_no(phase, i, j) + 2)
                    h = (0 if phase == "mem_a" else 2) + i
                    dve.tensor_copy(mkv[:, 0, h, :], ps_p[:, s, 0:MEM]).then_inc(evac[s], 1)

            mem_tile("mem_a", 0, 0, lambda: x_sums(2))
            mem_tile("mem_a", 0, 1, lambda: x_sums(3))
            mem_tile("mem_a", 1, 0, lambda: x_sums(0))
            mem_tile("mem_a", 1, 1, lambda: x_sums(1))
            dve.wait_ge(c_xe.sem, c_xe.at("xnorm", 0, 1))
            for n, (i, j) in enumerate(((0, 0), (0, 1), (1, 0), (1, 1))):
                mem_tile("mem_b", i, j, lambda: x_norm(n))
            dve.wait_ge(proj_done, TILE0["conv"] + 1)
            do(dve.memset(upad[:, :, 0:TAPS - 1], 0.0))
            do(tt(fg2[:, :], col("final_g", 0, KT), col("final_g", 0, KT), ALU.mult))
            l0, l1 = col("lower_bounds_2", 0, 8), col("lower_bounds_2", 8, 8)
            do(tt(hcol[:, 0, :], l0, l1, ALU.max))
            do(tt(hcol[:, 3, :], l0, hcol[:, 0, :], ALU.subtract))
            tt(hcol[:, 4, :], l1, hcol[:, 0, :], ALU.subtract).then_inc(conv_in, 1)

            def conv(i):
                s0, s1 = slot("conv", 0), slot("conv", 1)
                split("conv", i, 0)
                log_sigmoid("conv", i, 0, 1, wk[:, 0, :])
                dve.sem_inc(evac[s0], 1)
                split("conv", i, 1)
                dve.wait_ge(proj_done, tile_no("conv", i, 1) + 2)
                tt(upad[:, i, TAPS - 1:TAPS - 1 + S], ps_p[:, s1, :], wk[:, 0, :], ALU.mult).then_inc(evac[s1], 1)
            loop(dve, "conv", conv, order=o)

            o.settle()
            o.again()
            s = slot("flog", 0)
            dve.wait_ge(evac[slot("conv", 1)], half("conv", 3, 1) + 2)
            dve.sem_inc(conv_in, 1)
            split("flog", 0, 0)
            dve.wait_ge(c_ge.sem, c_ge.at("flog", 0, 1))
            do(ts(wk[0:NFOX, 2, :], ps_p[0:NFOX, s, :], cols[0:NFOX, COLS["b_f"][0]:COLS["b_f"][0] + 1], 0.0,
                  ALU.add, ALU.min))
            dve.sem_inc(evac[s], 1)
            dve.sem_inc(c_gu.sem, 1)
            do(tt(wk[0:NFOX, 2, :], wk[0:NFOX, 2, :], wk[0:NFOX, 1, :], ALU.subtract))
            do(dve.memset(wk[0:NFOX, 3, :], 1.0))
            dve.tensor_tensor_scan(cT[0:NFOX, :], wk[0:NFOX, 3, :], wk[0:NFOX, 2, :], 0.0, ALU.mult,
                                   ALU.add).then_inc(c_in.sem, 1)

            def silu_gate(phase, i, j, e, k=1):
                log_sigmoid(phase, i, j, k, e)
                do(tt(wk[:, 3, :], ps_p[:, slot(phase, j), :], e, ALU.mult))
                dve.sem_inc(evac[slot(phase, j)], 1)

            def memh(i):
                split("memh", i, 0)
                dve.wait_ge(proj_done, tile_no("memh", i, 0) + 2)
                dve.wait_ge(c_of.sem, c_of.at("memh", i, 0))
                do(ts(qkv[:, 0, :], ps_p[:, slot("memh", 0), :], SCALE, None, ALU.mult))
                dve.sem_inc(evac[slot("memh", 0)], 1)
                dve.sem_inc(c_qk.sem, 1)
                split("memh", i, 1)
                for b in range(2):
                    dve.wait_ge(c_sf.sem, c_sf.at("memh", i, b + 1))
                    do(dve.reduce_max(stat[:, 0, 2 * b:2 * b + 2],
                                      ps_s[:, b, :].rearrange("p (t m) -> p t m", t=2), AX_X))
                ts(stat[:, 1, :], stat[:, 0, :], -1.0, None, ALU.mult).then_inc(c_nm.sem, 1)
                dve.wait_ge(c_ex.sem, c_ex.at("memh", i, 1))
                do(dve.reciprocal(stat[:, 3, :], stat[:, 2, :]))
                for t in range(QT):
                    e = tp[:, 0, t * MEM:(t + 1) * MEM]
                    ins = ts(e, e, stat[:, 3, t:t + 1], None, ALU.mult)
                    if t < QT - 1:
                        o.step(ins)
                    else:
                        ins.then_inc(c_pr.sem, 1)
                silu_gate("memh", i, 1, wk[:, 0, :])
                dve.wait_ge(c_of.sem, c_of.at("memh", i, 1))
                tt(Y[:, 12 + i, :], ps_o[:, :], wk[:, 3, :], ALU.mult).then_inc(c_oe.sem, 1)
            loop(dve, "memh", memh, order=o)
            o.settle()
            o.again()

            def soft_in(phase, i, t, add):
                dve.wait_ge(c_sf.sem, c_sf.at(phase, i, t + 1))
                pr = (tp if phase == "fox" else tp2)[:, 0, :]
                e = pr[:, CAUSAL[t]:CAUSAL[t] + P * (t + 1)]
                add(t, e).then_inc(c_se.sem, 1)
                dve.wait_ge(c_se.sem, c_se.at(phase, i, t + 1))
                do(dve.reduce_max(stat[:, 0, t:t + 1], e, AX_X))
                ts(stat[:, 1, t:t + 1], stat[:, 0, t:t + 1], -1.0, None, ALU.mult).then_inc(c_nm.sem, 1)

            def soft_out(phase, i, t):
                dve.wait_ge(c_ex.sem, c_ex.at(phase, i, t + 1))
                do(dve.reciprocal(stat[:, 3, t:t + 1], stat[:, 2, t:t + 1]))
                pr = (tp if phase == "fox" else tp2)[:, 0, :]
                e = pr[:, CAUSAL[t]:CAUSAL[t] + P * (t + 1)]
                ins = ts(e, e, stat[:, 3, t:t + 1], None, ALU.mult)
                if t < QT - 1:
                    o.step(ins)
                else:
                    ins.then_inc(c_pr.sem, 1)

            dve.wait_ge(c_xe.sem, c_xe.at("cums", 0, 1))
            dve.wait_ge(c_ge.sem, c_ge.at("cums", 0, 1))
            stt(c_act[:, :], col("c_2", 0, KT), 0.0, c_act[:, :], ALU.min, ALU.subtract).then_inc(c_gu.sem, 1)
            dve.wait_ge(c_gs.sem, c_gs.at("cums", 0, 1))
            do(tt(c_act[:, :], c_act[:, :], col("c_2", 0, KT), ALU.mult))
            dve.sem_inc(ada_used, 1)

            def fox(i):
                def ada_step(n):
                    dve.wait_ge(s_ada[n % 2], 8 * 16 * i + 16 * (n // 2 + 1))
                    w, c = ada_ring[:, n % 2, :], c_act[:, n:n + 1]
                    if n == 0:
                        dve.wait_ge(c_xf.sem, c_xf.at("fox", i, 0))
                        ins = ts(ada_acc[:, :], w, c, None, ALU.mult)
                    else:
                        dve.wait_ge(ada_used, 16 * i + n + 1)
                        ins = stt(ada_acc[:, :], w, c, ada_acc[:, :], ALU.mult, ALU.add)
                    ins.then_inc(ada_used, 1)
                    if n == KT - 1:
                        dve.wait_ge(ada_used, 16 * i + n + 2)
                        dve.sem_inc(c_in.sem, 1)

                ts(wk[0:NFOX, 0, :], cT[0:NFOX, :], ident[0:NFOX, bass.ds(i, 1)], None, ALU.mult).then_inc(c_in.sem, 1)
                split("fox", i, 0)
                for n in range(4):
                    ada_step(n)
                dve.wait_ge(proj_done, tile_no("fox", i, 0) + 2)
                do(ts(qkv[:, 0, :], ps_p[:, slot("fox", 0), :], SCALE, None, ALU.mult))
                dve.sem_inc(evac[slot("fox", 0)], 1)
                split("fox", i, 1)
                for n in range(4, 10):
                    ada_step(n)
                dve.wait_ge(proj_done, tile_no("fox", i, 1) + 2)
                do(dve.tensor_copy(qkv[:, 1, :], ps_p[:, slot("fox", 1), :]))
                dve.sem_inc(evac[slot("fox", 1)], 1)
                dve.sem_inc(c_qk.sem, 1)
                split("fox", i, 2)
                dve.wait_ge(c_xe.sem, c_xe.at("fox", i, 1))
                for t in range(QT):
                    soft_in("fox", i, t, lambda t, e: stt(e, wk[:, 1, 0:P * (t + 1)], cn[:, t, bass.ds(i, 1)],
                                                          ps_s[:, t % 2, 0:P * (t + 1)], ALU.add, ALU.add))
                for t in range(QT):
                    soft_out("fox", i, t)
                split("fox", i, 3)
                for n in range(10, 16):
                    ada_step(n)
                silu_gate("fox", i, 3, wk[:, 2, :])
                dve.wait_ge(c_of.sem, c_of.at("fox", i, 1))
                tt(Y[:, 4 + i, :], ps_o[:, :], wk[:, 3, :], ALU.mult).then_inc(c_oe.sem, 1)
                dve.wait_ge(c_xf.sem, c_xf.at("fox", i, 3))
                tt(mod[:, bass.ds(6 * i, 6)], ps_x[:, 0:6],
                   cols[:, bass.ds(6 * i + COLS["b_ada_2"][0], 6)], ALU.add).then_inc(c_xe.sem, 1)
            loop(dve, "fox", fox, order=o)

            o.settle()
            o.again()
            dve.wait_ge(conv_out, 1)

            def conv_gate(j):
                log_sigmoid("gate", 0, j, j + 1, wk[:, 2, :])
                tt(tp[:, :, :].rearrange("p a n -> p (a n)")[:, j * S:(j + 1) * S], ps_p[:, slot("gate", j), :],
                   wk[:, 2, :], ALU.mult).then_inc(evac[slot("gate", j)], 1)
                dve.wait_ge(evac[slot("gate", j)], half("gate", 0, j) + 2)

            dve.sem_inc(c_in.sem, 1)
            split("gate", 0, 0)
            dve.wait_ge(c_xf.sem, c_xf.at("gate", 0, 1))
            do(ts(ssq_b[:, :], ps_x[:, :], 1.0 / (NCONV * P), None, ALU.mult))
            dve.sem_inc(c_xe.sem, 1)
            for c in range(NCONV):
                o.step(tt(Y[:, c, :], Y[:, c, :], ssq_b[:, :], ALU.subtract))
            o.settle()
            dve.sem_inc(c_ln.sem, 1)
            conv_gate(0)
            split("gate", 0, 1)
            dve.wait_ge(c_xe.sem, c_xe.at("gate", 0, 2))
            for c in range(NCONV):
                o.step(tt(Y[:, c, :], Y[:, c, :], r1[:, :], ALU.mult))
            o.settle()
            dve.sem_inc(c_ln.sem, 1)
            conv_gate(1)
            split("gate", 0, 2)
            for c in range(NCONV):
                dve.wait_ge(c_le.sem, c_le.at("gate", 0, c + 1))
                stt(qkv[:, c, :], Y[:, c, :], 0.0, qkv[:, c, :], ALU.min, ALU.subtract).then_inc(c_lu.sem, 1)
                dve.wait_ge(c_ls.sem, c_ls.at("gate", 0, c + 1))
                o.step(tt(qkv[:, c, :], qkv[:, c, :], Y[:, c, :], ALU.mult))
            o.settle()
            dve.sem_inc(c_uc.sem, 1)
            conv_gate(2)
            split("gate", 0, 3)
            conv_gate(3)

            lows = [0]

            def y_lo(order_):
                for k in order_:
                    lows[0] += 1
                    dve.wait_ge(moving_hi, 1 + 2 * KT + lows[0])
                    tt(act_lo[:, k, :], Y[:, k, :], act_hi[:, k, :].bitcast(F32), ALU.subtract).then_inc(moving, 1)

            y_lo(range(4, KT))
            for m in range(NCONV):
                dve.wait_ge(c_pf.sem, c_pf.at("pw", 0, m + 1))
                bank = (ps_s[:, 0, :], ps_s[:, 1, :], ps_t[:, 0, :], ps_t[:, 1, :])[m]
                tt(Y[:, m, :], bank, tp[:, :, :].rearrange("p a n -> p (a n)")[:, m * S:(m + 1) * S],
                   ALU.mult).then_inc(c_yc.sem, 1)
                y_lo([m])
            do(dve.memset(ssq_a[:, :], 0.0))
            do(dve.memset(ssq_b[:, :], 0.0))
            dve.wait_ge(lb_exp, 1)
            do(tt(hcol[:, 5, :], hcol[:, 3, :], hcol[:, 4, :], ALU.add))
            do(dve.reciprocal(hcol[:, 5, :], hcol[:, 5, :]))
            do(tt(hcol[:, 0, :], hcol[:, 3, :], hcol[:, 5, :], ALU.mult))
            do(ts(hcol[:, 1, :], hcol[:, 0, :], -1.0, 1.0, ALU.mult, ALU.add))
            do(ts(hcol[:, 2, :], hcol[:, 0, :], LB_LEAST, None, ALU.max))
            do(ts(gall[:, :], mod[:, KT:2 * KT], 1.0, None, ALU.add))
            do(tt(gall[:, :], gall[:, :], col("norm_g_2", 0, KT), ALU.mult))
            do(tt(gall[:, :], gall[:, :], col("final_g", 0, KT), ALU.mult))
            do(ts(hcol[:, 6, 0:1], col("q_norm_g_2"), SCALE, None, ALU.mult))

            def out1(i):
                for j in range(2):
                    s = slot("out1", j)
                    split("out1", i, j)
                    dve.wait_ge(proj_done, tile_no("out1", i, j) + 2)
                    dve.wait_ge(s_stage[j], 16 * i + 16)
                    o.step(tt(Y[:, 2 * i + j, :], ps_p[:, s, :], stage1[:, j, :], ALU.add))
                    o.settle()
                    dve.sem_inc(evac[s], 1)
                    dve.sem_inc(c_tt.sem, 1)
                    dve.wait_ge(c_sq.sem, c_sq.at("out1", i, j + 1))
                    o.step(tt(ssq_a[:, :], ssq_a[:, :], wk[:, j, :], ALU.add))
                    o.step(stt(ssq_b[:, :], wk[:, j, :], fg2[:, bass.ds(2 * i + j, 1)], ssq_b[:, :], ALU.mult, ALU.add))
                    o.settle()
            loop(dve, "out1", out1, order=o)
            o.settle()
            o.again()
            dve.sem_inc(c_in.sem, 1)
            dve.wait_ge(c_r2.sem, c_r2.at("norm2", 0, 1))
            do(tt(wk[:, 3, :], ps_o[:, :], r1[:, :], ALU.mult))
            dve.sem_inc(c_xe.sem, 1)
            tt(wk[:, 3, :], wk[:, 3, :], r1[:, :], ALU.mult).then_inc(c_m2.sem, 1)
            dve.wait_ge(c_r2.sem, c_r2.at("norm2", 0, 2))
            do(tt(wk[:, 2, :], wk[:, 2, :], r1[:, :], ALU.mult))

            def h_lo(k):
                dve.wait_ge(moving_hi, 1 + 3 * KT + k + 1)
                stt(act_lo[:, k, :], wk[:, k % 2, :], mod[:, k:k + 1], act_hi[:, k, :].bitcast(F32), ALU.add,
                    ALU.subtract).then_inc(moving, 1)

            for k in range(KT):
                if k >= 2:
                    dve.wait_ge(moving, 1 + 2 * KT + k - 1)
                stt(wk[:, k % 2, :], Y[:, k, :], gall[:, k:k + 1], wk[:, 2, :], ALU.mult, ALU.mult).then_inc(
                    c_u2.sem, 1)
                if k:
                    h_lo(k - 1)
            h_lo(KT - 1)
            for j in range(2):
                dve.wait_ge(s_store[j], 16 * 8)

            def att(i):
                def normed(j, gcol):
                    dve.wait_ge(c_rr.sem, c_rr.at("att", i, j + 1))
                    s = slot("att", j)
                    do(stt(qkv2[:, j, :], ps_p[:, s, :], gcol, wk[:, 1, :], ALU.mult, ALU.mult))
                    dve.sem_inc(evac[s], 1)
                    if j:
                        dve.sem_inc(c_qk.sem, 1)

                def add_bias(t, e):
                    w = P * (t + 1)
                    n = min(w, 2 * P)
                    if w > n:
                        o.step(ts(e[:, 0:w - n], ps_s[:, t % 2, 0:w - n], bt[:, 2 * P:2 * P + 1], None, ALU.add))
                    return tt(e[:, w - n:w], ps_s[:, t % 2, w - n:w], bt[:, 2 * P - n:2 * P], ALU.add)

                split("att", i, 0)
                split("att", i, 1)
                normed(0, hcol[:, 6, 0:1])
                split("att", i, 2)
                normed(1, col("k_norm_g_2"))
                dve.wait_ge(s_bias, 16 * i + 16)
                for t in range(3):
                    soft_in("att", i, t, add_bias)
                for t in range(2):
                    soft_out("att", i, t)
                split("att", i, 3)
                soft_in("att", i, 3, add_bias)
                dve.wait_ge(c_nm.sem, c_nm.at("att", i, 4))
                dve.sem_inc(c_bt.sem, 1)
                for t in range(2, QT):
                    soft_out("att", i, t)
                silu_gate("att", i, 3, wk[:, 2, :])
                dve.wait_ge(c_of.sem, c_of.at("att", i, 1))
                tt(Y[:, i, :], ps_o[:, :], wk[:, 3, :], ALU.mult).then_inc(c_oe.sem, 1)
            loop(dve, "att", att, order=o)
            o.settle()
            o.again()
            do(dve.memset(hA[:, :, :], 0.0))

            def blocks(ap, n):
                return ap.rearrange("p (b n) -> p b n", n=n)

            def hg(i):
                s = slot("hg", 0)
                split("hg", i, 0)
                dve.wait_ge(c_ge.sem, c_ge.at("hg", i, 1))
                o.step(stt(wk[:, 0, :], ps_p[:, s, :], 0.0, wk[:, 1, :], ALU.min, ALU.subtract))
                o.step(stt(wk[:, 1, :], ps_p[:, s, :], 0.0, wk[:, 1, :], ALU.max, ALU.add))
                o.settle()
                dve.sem_inc(evac[s], 1)
                dve.sem_inc(c_gu.sem, 1)
                split("hg", i, 1)
                dve.wait_ge(c_gs.sem, c_gs.at("hg", i, 1))
                do(ts(hk, hk, hcol[:, 1, bass.ds(i, 1)], None, ALU.mult))
                dve.wait_ge(c_lf.sem, c_lf.at("hg", i, 1))
                dve.tensor_tensor_scan(hb[:, :], starts, hd[:, 0, :], 0.0, ALU.mult, ALU.add).then_inc(c_b.sem, 1)
                dve.wait_ge(c_b.sem, c_b.at("hg", i, 1))

                def diff(n):
                    width, ref = (CHUNK, CHUNK - 1) if n == 0 else (2 * HALVES[n - 1], HALVES[n - 1] - 1)
                    if n >= 2:
                        dve.wait_ge(c_dz.sem, c_dz.at("hg", i, n - 1))
                    b = blocks(hb[:, :], width)
                    r = b[:, :, ref:ref + 1].broadcast_to([P, S // width, width])
                    tt(blocks(hd[:, n % 2, :], width), b, r, ALU.subtract).then_inc(c_dd.sem, 1)

                diff(0)
                diff(1)
                log_sigmoid("hg", i, 1, 2, wk[:, 3, :])
                s = slot("hg", 1)
                o.step(tt(hq[:, :], ps_p[:, s, :], wk[:, 3, :], ALU.mult))
                o.settle()
                dve.sem_inc(evac[s], 1)
                dve.sem_inc(c_qr.sem, 1)
                split("hg", i, 2)

                def masked(n):
                    dve.wait_ge(c_sf.sem, c_sf.at("hg", i, n + 1))
                    o.note()
                    o.settle()
                    dve.copy_predicated(hA[:, :, :], levels[:, n:n + 1, :].broadcast_to([P, QT, P]),
                                        ps_s[:, n % 2, :].rearrange("p (t n) -> p t n", t=QT)).then_inc(c_se.sem, 1)
                    dve.wait_ge(c_se.sem, c_se.at("hg", i, n + 1))
                diff(2)
                masked(0)
                for n in range(3, NLEV):
                    diff(n)
                    masked(n - 2)
                masked(NLEV - 2)
                masked(NLEV - 1)
                dve.sem_inc(c_A.sem, 1)
                split("hg", i, 3)
                dve.wait_ge(c_eb.sem, c_eb.at("hg", i, 1))
                dve.wait_ge(c_kvf.sem, c_kvf.at("hg", i, 1))
                do(dve.tensor_copy(hS[:, 0, :], ps_t[:, 0, 0:P]))
                for n in range(1, NCH - 1):
                    if n == 1:
                        dve.wait_ge(c_kvf.sem, c_kvf.at("hg", i, 2))
                    last = n * CHUNK + CHUNK - 1
                    do(stt(hS[:, n, :], hS[:, n - 1, :], heb[:, last:last + 1],
                           ps_t[:, n % 2, n // 2 * P:(n // 2 + 1) * P], ALU.mult, ALU.add))
                dve.sem_inc(c_st.sem, 1)
                silu_gate("hg", i, 3, wk[:, 2, :], 3)
                dve.wait_ge(c_rr.sem, c_rr.at("hg", i, 1))
                do(stt(wk[:, 2, :], ps_o[:, :], col("hg_norm_g_2"), ssq_a[:, :], ALU.mult, ALU.mult))
                tt(Y[:, 8 + i, :], wk[:, 2, :], wk[:, 3, :], ALU.mult).then_inc(c_oe.sem, 1)
                dve.wait_ge(c_oe.sem, c_oe.at("hg", i, 1))
            loop(dve, "hg", hg, order=o)
            o.settle()
            o.again()
            for k in range(KT):
                dve.wait_ge(moving_hi, 1 + 4 * KT + k + 1)
                tt(act_lo[:, k, :], Y[:, k, :], act_hi[:, k, :].bitcast(F32), ALU.subtract).then_inc(moving, 1)

            def out2(i):
                for j in range(2):
                    s = slot("out2", j)
                    split("out2", i, j)
                    dve.wait_ge(s_stage[j], 16 * 8 + 16 * i + 16)
                    dve.wait_ge(s_store[j], 16 * 8 + 16 * i)
                    do(stt(wk[:, j, :], stage2[:, j, :], cols[:, bass.ds(2 * i + (COLS["final_g"][0] + j), 1)], r1[:, :],
                           ALU.mult, ALU.mult))
                    dve.wait_ge(proj_done, tile_no("out2", i, j) + 2)
                    o.step(stt(wk[:, j, :], ps_p[:, s, :], mod[:, bass.ds(2 * i + (2 * KT + j), 1)], wk[:, j, :],
                               ALU.mult, ALU.add))
                    o.settle()
                    dve.sem_inc(evac[s], 1)
                    dve.sem_inc(s_out, 1)
            loop(dve, "out2", out2, peel=1, order=o)

        @block.gpsimd
        def _(pool):
            o = Order(pool, own["pool"])
            tt = pool.tensor_tensor
            pool.wait_ge(s_const, 48)
            pool.wait_ge(conv_in, 2)
            for c in range(NCONV):
                o.step(pool.tensor_copy(Y[:, c, :], col("conv_b", c).broadcast_to([P, S])))
            o.settle()
            with pool.Fori(0, TAPS) as tap:
                o.again()
                for c in range(NCONV):
                    w0 = COLS["conv_w"][0] + c * TAPS
                    o.step(tt(ctmp[:, :], upad[:, c, bass.ds(tap, S)],
                              cols[:, bass.ds(tap + w0, 1)].broadcast_to([P, S]), ALU.mult))
                    o.settle()
                    o.step(tt(Y[:, c, :], Y[:, c, :], ctmp[:, :], ALU.add))
                    o.settle()
            pool.sem_inc(conv_out, 1)

            def hg(i):
                for n in range(NLEV):
                    pool.wait_ge(c_de.sem, c_de.at("hg", i, n + 1))
                    if n == 0:
                        pool.wait_ge(c_xf.sem, c_xf.at("hg", i, 0))
                        o.step(tt(hkd[:, :], hk[:, :], hd[:, 0, :], ALU.mult))
                        o.settle()
                        pool.sem_inc(c_dz.sem, 1)
                        pool.wait_ge(c_qr.sem, c_qr.at("hg", i, 1))
                        pool.wait_ge(c_eb.sem, c_eb.at("hg", i, 1))
                        pool.wait_ge(c_of.sem, c_of.at("hg", i, 0))
                        tt(hqd[:, :], hq[:, :], heb[:, :], ALU.mult).then_inc(c_qd.sem, 1)
                        continue
                    h = HALVES[n - 1]
                    if n >= 3:
                        pool.wait_ge(c_sf.sem, c_sf.at("hg", i, n - 1))
                    z = hz[:, (n - 1) % 2, :].rearrange("p (b n) -> p b n", n=2 * h)
                    d = hd[:, n % 2, :].rearrange("p (b n) -> p b n", n=2 * h)
                    k = hk[:, :].rearrange("p (b n) -> p b n", n=2 * h)
                    q = hq[:, :].rearrange("p (b n) -> p b n", n=2 * h)
                    o.step(tt(z[:, :, 0:h], k[:, :, 0:h], d[:, :, 0:h], ALU.mult))
                    tt(z[:, :, h:2 * h], q[:, :, h:2 * h], d[:, :, h:2 * h], ALU.mult).then_inc(c_dz.sem, 1)
            loop(pool, "hg", hg, order=o)
            pool.wait_ge(c_dz.sem, c_dz.at("hg", 7, 7))


def _tiles(np, w, starts):
    out = np.zeros((len(starts), P, KT, P), np.float32)
    for n, s in enumerate(starts):
        c = w[:, s:min(s + P, w.shape[1])] if not isinstance(s, tuple) else w[:, s[0]:s[1]]
        out[n, :, :, :c.shape[1]] = c.reshape(KT, P, c.shape[1]).transpose(1, 0, 2)
    return out.reshape(len(starts), P, D)


def kernel(**inputs):
    import numpy as np
    import concourse.bacc as _bacc
    from concourse import mybir as _mybir
    from concourse.bass_utils import run_bass_kernel_spmd as _run

    a = {k: np.asarray(v) for k, v in inputs.items()}
    w1, wkv, wo1 = a["w_in"][0], a["w_mem_kv"][0], a["w_out"][0]
    w2, wo2 = a["w_in_2"][0], a["w_out_2"][0]
    CW, FW = NCONV * P, NFOX * P
    fq, fk, fv, fl = 3 * CW, 3 * CW + FW, 3 * CW + 2 * FW, 3 * CW + 3 * FW
    fg, mq = fl + NFOX, fl + NFOX + FW
    mg = mq + NMEMH * P
    mv = NMEMH * P
    first = [t for i in range(4) for t in (CW + i * P, i * P)]
    first += [(fl, fl + NFOX)]
    first += [t for h in range(NMEMH) for t in (mq + h * P, mg + h * P)]
    first += [t for h in range(NFOX) for t in (fq + h * P, fk + h * P, fv + h * P, fg + h * P)]
    first += [2 * CW + i * P for i in range(4)]
    AW = NATT * P
    second = [t + h * P for h in range(NATT) for t in (0, AW, 2 * AW, 3 * AW)]
    second += [t + h * P for h in range(NHG) for t in (5 * AW, 4 * AW, 6 * AW, 7 * AW)]
    wt = np.concatenate([
        _tiles(np, wkv, [t for h in range(NMEMH) for t in (mv + h * P, h * P)]),
        _tiles(np, w1, first), _tiles(np, wo1, [m * P for m in range(KT)]),
        _tiles(np, w2, second), _tiles(np, wo2, [m * P for m in range(KT)])])
    assert wt.shape[0] == NTILES

    def along(v, n):
        return v.reshape(n, P).T

    cols = np.zeros((P, NCOLS), np.float32)

    def put(name, v):
        c, n = COLS[name]
        cols[:, c:c + n] = v
    for name in ("norm_g", "mem_norm_g", "norm_g_2", "c_2"):
        put(name, along(a[name][0], KT))
    put("final_g", along(a["final_g"], KT))
    put("b_ada_2", along(a["b_ada_2"][0], 48))
    put("conv_w", a["conv_w"][0].reshape(TAPS, NCONV, P).transpose(2, 1, 0).reshape(P, NCONV * TAPS))
    for name in ("conv_b", "conv_ln_g", "conv_ln_b"):
        put(name, along(a[name][0], NCONV))
    for name in ("q_norm_g_2", "k_norm_g_2", "hg_norm_g_2"):
        put(name, along(a[name][0], 1))
    put("lower_bounds_2", a["lower_bounds_2"].reshape(2, NHG, P).transpose(2, 0, 1).reshape(P, 2 * NHG))
    cols[0:NFOX, COLS["b_f"][0]] = a["b_f"][0]
    put("one", 1.0)
    put("eps", EPS)

    n = np.arange(P)
    consts = np.zeros((P, CONSTS), np.float32)
    consts[:, 0:P] = 1.0
    consts[:, P:2 * P] = np.eye(P)
    consts[:, 2 * P:] = (np.arange(S) % CHUNK != 0)[None, :]
    masks = np.zeros((P, 3 + NLEV, P), np.float32)
    masks[:, 0] = np.eye(P)
    masks[:, 1] = np.where(n[None, :] > n[:, None], NEG, 0.0)
    masks[:, 2] = np.where(n[None, :] // CHUNK > n[:, None] // CHUNK, NEG, 0.0)
    masks[:, 3] = np.eye(P)
    for m, h in enumerate(HALVES):
        s, t = n[:, None], n[None, :]
        masks[:, m + 4] = (s // (2 * h) == t // (2 * h)) & (s % (2 * h) < h) & (t % (2 * h) >= h)

    masks = masks.astype(_mybir.dt.np(BF16))

    rel = a["rel_bias_2"][0]
    dist = P + n[:, None] - np.arange(2 * P)[None, :]
    bias = np.empty((NATT, P, 2 * P + 1), np.float32)
    bias[:, :, 0:2 * P] = rel[:, np.minimum(dist, P) + P]
    bias[:, :, 2 * P] = rel[:, 2 * P][:, None]

    arrays = {
        "wt": wt,
        "ada": a["w_ada_2"][0].reshape(KT, P, NFOX, ADA_COLS).transpose(2, 0, 1, 3),
        "bias": bias,
        "xT": a["x"][0].T.reshape(KT, P, S).transpose(1, 0, 2),
        "memT": a["mem"][0].T.reshape(KT, P, MEM).transpose(1, 0, 2).reshape(P, KT * MEM),
        "pw": a["w_conv_pw"][0].reshape(NCONV, P, CW).transpose(1, 0, 2),
        "cols": cols, "consts": consts, "masks": masks,
    }
    arrays = {f"{k}_dram": np.ascontiguousarray(v) for k, v in arrays.items()}
    nc = _bacc.Bacc("TRN2", target_bir_lowering=False, num_devices=1)
    args = [nc.dram_tensor(k, v.shape, _mybir.dt.from_np(v.dtype), kind="ExternalInput").ap()
            for k, v in arrays.items()]
    args.append(nc.dram_tensor("spill_dram", (KT, P, S), F32, kind="Internal").ap())
    args.append(nc.dram_tensor("out_dram", (KT, P, S), F32, kind="ExternalOutput").ap())
    build(nc, *args)
    r = _run(nc, [arrays], core_ids=[0])
    got = r.results[0]["out_dram"]
    return np.ascontiguousarray(np.asarray(got).reshape(D, S).T)[None]
```

```python
from contextlib import ExitStack

import concourse.bass as bass
from concourse import mybir

ALU = mybir.AluOpType
ACT = mybir.ActivationFunctionType
AX_X = mybir.AxisListType.X
F32 = mybir.dt.float32
F32R = mybir.dt.float32r
BF16 = mybir.dt.bfloat16
U16 = mybir.dt.uint16

P = 128
D = 2048
KT = D // P
S = 512
QT = S // P
MEM = 256
MT = MEM // P
CHUNK = 64
NCH = S // CHUNK
HALVES = (32, 16, 8, 4, 2, 1)
NLEV = len(HALVES) + 1
TAPS = 31
NCONV = 4
NMEMH = 4
NFOX = 8
NATT = 8
NHG = 8
ADA = dict(fox=(4, 2), out1=(2, 4))
ADA_PIECE = 8 * P
ADA_AT = dict(fox=(3, 3, 0, 2), out1=(2, 2))
ADA_G0 = dict(fox=0, out1=64)
ADA_M0 = dict(fox=0, out1=32)
ADA_PIECES = 96
EPS = 1e-6
SCALE = float(P) ** -0.5
LB_LEAST = 1e-19
NEG = -1e30

PHASES = {
    "start": (1, 0),
    "mem_a": (2, 2),
    "xnorm": (1, 0),
    "mem_b": (2, 2),
    "conv": (4, 2),
    "flog": (1, 1),
    "memh": (4, 2),
    "cums": (1, 0),
    "fox": (8, 4),
    "gate": (1, 4),
    "pw": (1, 0),
    "out1": (8, 2),
    "norm2": (1, 0),
    "att": (8, 4),
    "hg": (8, 4),
    "out2": (8, 2),
}
TILE0 = {}
_t = 0
for _name, (_n, _w) in PHASES.items():
    TILE0[_name] = _t
    _t += _n * _w
NTILES = _t

COLS = {}
_c = 0
for _name, _n in (("norm_g", 16), ("mem_norm_g", 16), ("final_g", 16), ("norm_g_2", 16), ("c_2", 16),
                  ("b_ada_2", 48), ("conv_w", NCONV * TAPS), ("conv_b", 4), ("conv_ln_g", 4), ("conv_ln_b", 4),
                  ("q_norm_g_2", 1), ("k_norm_g_2", 1), ("hg_norm_g_2", 1), ("lower_bounds_2", 16), ("b_f", 1),
                  ("one", 1), ("eps", 1)):
    COLS[_name] = (_c, _n)
    _c += _n
NCOLS = _c

CONSTS = 2 * P + S


class Count:

    def __init__(self, sem, **per):
        self.sem, self.base, self.per = sem, {}, {}
        n = 0
        for name, (iters, _) in PHASES.items():
            self.base[name], self.per[name] = n, per.get(name, 0)
            n += iters * per.get(name, 0)

    def at(self, phase, i, k):
        return self.per[phase] * i + (1 + self.base[phase] + k)


class Order:

    def __init__(self, eng, sem):
        self.eng, self.sem, self.n = eng, sem, 0

    def step(self, ins):
        self.n += 1
        ins.then_inc(self.sem, 1)

    def settle(self):
        if self.n:
            self.eng.wait_ge(self.sem, self.n)

    def note(self):
        self.n += 1
        self.eng.sem_inc(self.sem, 1)

    def again(self):
        self.eng.sem_clear(self.sem)
        self.n = 0


def build(nc, wt, ada, bias, xT, memT, pw, cols_d, consts_d, masks_d, spill, out):
    ctx = ExitStack()
    with ctx:
        def sb(name, shape, dt=F32, stack=ctx):
            return stack.enter_context(nc.sbuf_tensor(name, shape, dt))

        def sem(name):
            return ctx.enter_context(nc.semaphore(name))

        act_hi = sb("act_hi", [P, KT, S], F32R)
        act_lo = sb("act_lo", [P, KT, S], F32R)
        Y = sb("Y", [P, KT, S])
        raw = sb("raw", [P, 2, D])
        w_hi = sb("w_hi", [P, 2, D], F32R)
        w_lo = sb("w_lo", [P, 2, D], F32R)
        cols = sb("cols", [P, NCOLS])
        consts = sb("consts", [P, CONSTS])
        masks = sb("masks", [P, 3 + NLEV, P], BF16)
        levels = masks[:, 3:3 + NLEV, :].bitcast(U16)
        mod = sb("mod", [P, 48])
        c_act = sb("c_act", [P, KT])
        gall = sb("gall", [P, KT])
        hcol = sb("hcol", [P, 8, NHG])
        cn = sb("cn", [P, QT, NFOX])
        stat = sb("stat", [P, 6, QT])
        ssq_a = sb("ssq_a", [P, S])
        ssq_b = sb("ssq_b", [P, S])
        r1 = sb("r1", [P, S])
        wk = sb("wk", [P, 4, S])
        ones, ident, starts = consts[:, 0:P], consts[:, P:2 * P], consts[:, 2 * P:2 * P + S]
        eye_b, causal_b, chunk_b = masks[:, 0, :], masks[:, 1, :], masks[:, 2, :]

        def col(name, k=0, n=1):
            return cols[:, COLS[name][0] + k:COLS[name][0] + k + n]

        memv = Y[:, 0:8, :].rearrange("p k s -> p (k s)").rearrange("p (k m) -> p k m", k=KT)
        x_ring = (wk[:, 0, :], wk[:, 1, :], ssq_b[:, :])
        h_ring = ((wk[:, 0, :], ssq_a[:, :]), (wk[:, 1, :], wk[:, 3, :]))
        one_c, eps_c = col("one"), col("eps")

        mkv = sb("mkv", [P, 2, NMEMH, MEM])
        ada_ring = mkv[:, :, :, :].rearrange("p a h m -> p a (h m)")
        with ExitStack() as early:
            mem_hi = sb("mem_hi", [P, KT, MEM], F32R, early)
            mem_lo = sb("mem_lo", [P, KT, MEM], F32R, early)
        first = ExitStack()
        qkv = sb("qkv", [P, 4, S], F32, first)
        tp = sb("tp", [P, 2, 1280], F32, first)
        upad = sb("upad", [P, NCONV, TAPS - 1 + S], F32, first)
        pwt = upad[:, :, 0:S]
        ctmp = sb("ctmp", [P, S], F32, first)
        ada_acc = sb("ada_acc", [P, S], F32, first)
        cT = sb("cT", [P, S], F32, first)
        stage1 = qkv[:, 0:2, :]
        first.close()
        second = ExitStack()
        qkv2 = sb("qkv2", [P, 4, S], F32, second)
        tp2 = sb("tp2", [P, 2, 1280], F32, second)
        bt = sb("bt", [P, 2 * P + 1], F32, second)
        second.close()
        third = ExitStack()
        hqk = sb("hqk", [P, 2, S], F32, third)
        hq, hk, stage2 = hqk[:, 0, :], hqk[:, 1, :], hqk
        hb = sb("hb", [P, S], F32, third)
        heb = sb("heb", [P, S], F32, third)
        hqd = sb("hqd", [P, S], F32, third)
        hkd = sb("hkd", [P, S], F32, third)
        hz = sb("hz", [P, 2, S], F32, third)
        hd = sb("hd", [P, 2, S], F32, third)
        hvT = sb("hvT", [P, S], F32, third)
        hvn = sb("hvn", [P, QT, P], F32, third)
        hkn = sb("hkn", [P, QT, P], F32, third)
        hA = sb("hA", [P, QT, P], F32, third)
        hS = sb("hS", [P, NCH - 1, P], F32, third)
        third.close()

        ps_p = ctx.enter_context(nc.psum_tensor("ps_p", [P, 2, S], F32))
        ps_s = ctx.enter_context(nc.psum_tensor("ps_s", [P, 2, S], F32))
        ps_t = ctx.enter_context(nc.psum_tensor("ps_t", [P, 2, S], F32))
        ps_o = ctx.enter_context(nc.psum_tensor("ps_o", [P, S], F32))
        ps_x = ctx.enter_context(nc.psum_tensor("ps_x", [P, S], F32))

        s_const = sem("s_const")
        s_cols = sem("s_cols")
        s_mem = [sem(f"s_mem{n}") for n in range(4)]
        s_x = [sem(f"s_x{n}") for n in range(4)]
        s_raw = [sem("s_raw0"), sem("s_raw1")]
        s_ada = [sem("s_ada0"), sem("s_ada1")]
        s_stage = [sem("s_stage0"), sem("s_stage1")]
        s_bias = sem("s_bias")
        s_pw = sem("s_pw")
        s_store = [sem("s_store0"), sem("s_store1")]
        w_hi_done = sem("w_hi_done")
        w_split = sem("w_split")
        proj_done = sem("proj_done")
        evac = [sem("evac0"), sem("evac1")]
        mem_split = sem("mem_split")
        moving = sem("moving")
        moving_hi = sem("moving_hi")
        conv_in = sem("conv_in")
        conv_out = sem("conv_out")
        ada_used = sem("ada_used")
        sqs = sem("sqs")
        mem_sq = sem("mem_sq")
        mem_added = sem("mem_added")
        sq_x = sem("sq_x")
        sq_y = sem("sq_y")
        heads = dict(memh=1, fox=1, att=1)
        qk_ready = Count(sem("qk_ready"), **heads)
        scores_full = Count(sem("scores_full"), memh=2, fox=4, att=4, hg=NLEV)
        scores_free = Count(sem("scores_free"), memh=2, fox=4, att=4, hg=NLEV)
        max_ready = Count(sem("max_ready"), memh=1, fox=4, att=4)
        exp_done = Count(sem("exp_done"), memh=1, fox=4, att=4)
        probs_ready = Count(sem("probs_ready"), **heads)
        probsT_full = Count(sem("probsT_full"), memh=2, fox=4, att=4)
        probsT_ready = Count(sem("probsT_ready"), memh=2, fox=4, att=4)
        value_ready = Count(sem("value_ready"), mem_a=1, mem_b=1, memh=1, fox=1, att=1, hg=1)
        heads_full = Count(sem("heads_full"), memh=1, fox=1, att=1, hg=1)
        heads_done = Count(sem("heads_done"), memh=1, fox=1, att=1, hg=1)
        gates = dict(conv=1, flog=1, memh=1, cums=1, fox=1, gate=4, att=1, hg=3)
        gate_soft = Count(sem("gate_soft"), **gates)
        gate_log = Count(sem("gate_log"), **gates)
        gate_sig = Count(sem("gate_sig"), **gates)
        side_full = Count(sem("side_full"), start=1, mem_a=1, xnorm=1, mem_b=1, cums=1, fox=3, gate=2, out1=1,
                     norm2=1, att=3, hg=3)
        side_free = Count(sem("side_free"), start=1, mem_a=1, xnorm=1, mem_b=1, cums=1, fox=3, gate=2, out1=1,
                     norm2=1, att=3, hg=3)
        side_in = Count(sem("side_in"), xnorm=2, cums=1, fox=2, gate=2, out1=1, att=2, hg=1)
        ln_ready = Count(sem("ln_ready"), gate=4)
        ln_soft = Count(sem("ln_soft"), gate=4)
        ln_log = Count(sem("ln_log"), gate=4)
        ln_sig = Count(sem("ln_sig"), gate=4)
        lb_exp = sem("lb_exp")
        pw_in = Count(sem("pw_in"), gate=1)
        pw_full = Count(sem("pw_full"), pw=4)
        pw_done = Count(sem("pw_done"), pw=4)
        squares_ready = Count(sem("squares_ready"), out1=4)
        squares_added = Count(sem("squares_added"), out1=2)
        residual_tile = Count(sem("residual_tile"), out1=2)
        norm2_tiles = Count(sem("norm2_tiles"), norm2=16)
        norm2_rows = Count(sem("norm2_rows"), norm2=3)
        norm2_mean = Count(sem("norm2_mean"), norm2=1)
        rms_rows = Count(sem("rms_rows"), att=2, hg=1)
        bias_used = Count(sem("bias_used"), att=1)
        forget_log = Count(sem("forget_log"), hg=1)
        decay_ready = Count(sem("decay_ready"), hg=1)
        decay_exp = Count(sem("decay_exp"), hg=1)
        level_diff = Count(sem("level_diff"), hg=7)
        level_exps = Count(sem("level_exps"), hg=7)
        query_ready = Count(sem("query_ready"), hg=1)
        level_in = Count(sem("level_in"), hg=7)
        query_decayed = Count(sem("query_decayed"), hg=1)
        scores_masked = Count(sem("scores_masked"), hg=1)
        kv_full = Count(sem("kv_full"), hg=2)
        states_ready = Count(sem("states_ready"), hg=1)
        s_out = sem("s_out")
        h_full = sem("h_full")
        h_odd = sem("h_odd")
        credited = [w_hi_done, w_split, proj_done, *evac, moving, moving_hi] + [
            c.sem for c in (
                qk_ready, scores_full, scores_free, max_ready, exp_done, probs_ready, probsT_full,
                probsT_ready, value_ready, heads_full, heads_done, gate_soft, gate_log, gate_sig,
                side_full, side_free, side_in, ln_ready, ln_soft, ln_log, ln_sig, pw_in, pw_full,
                pw_done, squares_ready, squares_added, residual_tile, norm2_tiles, norm2_rows,
                norm2_mean, rms_rows, bias_used, forget_log, decay_ready, decay_exp, level_diff,
                level_exps, query_ready, level_in, query_decayed, scores_masked, kv_full, states_ready)]
        own = {n: sem(f"own_{n}") for n in ("act", "dve", "pool")}

        CAUSAL = [128 * i * (i + 1) // 2 for i in range(QT)]
        CAUSAL_T = [0, 512, 896, 1152]

        def blocks(ap, n):
            return ap.rearrange("p (b n) -> p b n", n=n)

        def right_halves(ap, h):
            if len(ap.shape) == 2:
                return blocks(ap, 2 * h)[:, :, h:2 * h]
            return ap.rearrange("p t (b n) -> p t b n", n=2 * h)[:, :, :, h:2 * h]

        def tile_no(phase, i, j):
            return PHASES[phase][1] * i + (TILE0[phase] + j)

        def half(phase, i, j):
            return PHASES[phase][1] // 2 * i + (TILE0[phase] + j) // 2

        def slot(phase, j):
            return (TILE0[phase] + j) % 2

        def loop(eng, phase, body, peel=0, head=0, order=None):
            n = PHASES[phase][0]

            def once(i):
                if order is not None:
                    order.again()
                body(i)
                if order is not None:
                    order.settle()

            if order is not None:
                order.settle()
            for i in range(head):
                once(i)
            if n - peel - head > 1:
                with eng.Fori(head, n - peel) as i:
                    once(i)
            else:
                peel = n - head
            for i in range(n - peel, n):
                once(i)

        block = ctx.enter_context(nc.Block())

        @block.sync
        def _(sp):
            for c in credited:
                sp.sem_inc(c, 1)
            sp.dma_start(cols[:, :], cols_d).then_inc(s_cols, 16)
            sp.dma_start(raw[:, 0, :], wt[0]).then_inc(s_raw[0], 16)
            for n in range(4):
                sp.dma_start(Y[:, 2 * n:2 * n + 2, :], memT[:, 2 * n:2 * n + 2, :]).then_inc(s_mem[n], 16)
            sp.dma_start(raw[:, 1, :], wt[1]).then_inc(s_raw[1], 16)
            sp.dma_start(consts[:, :], consts_d).then_inc(s_const, 16)
            sp.dma_start(masks[:, :, :], masks_d).then_inc(s_const, 16)
            for g in (2, 3):
                sp.dma_start(Y[:, 4 * g:4 * g + 4, :], xT[:, 4 * g:4 * g + 4, :]).then_inc(s_x[g], 16)

            def load(phase, i, j, ahead=3):
                t = tile_no(phase, i, j)
                if isinstance(t, int) and t + ahead >= NTILES:
                    return
                sp.wait_ge(w_split, t + ahead)
                s = (TILE0[phase] + j + ahead) % 2
                sp.dma_start(raw[:, s, :], wt[t + ahead]).then_inc(s_raw[s], 16)

            load("start", 0, 0, 2)
            sp.wait_ge(mem_split, KT)
            sp.wait_ge(sqs, KT)
            sp.wait_ge(mem_sq, KT)
            for g in (0, 1):
                sp.dma_start(Y[:, 4 * g:4 * g + 4, :], xT[:, 4 * g:4 * g + 4, :]).then_inc(s_x[g], 16)
            for phase in ("mem_a", "mem_b", "conv"):
                loop(sp, phase, lambda i: [load(phase, i, j) for j in range(2)])
            load("flog", 0, 0)
            loop(sp, "memh", lambda i: [load("memh", i, j) for j in range(2)])
            sp.wait_ge(value_ready.sem, value_ready.at("memh", 3, 1))
            sp.wait_ge(scores_full.sem, scores_full.at("memh", 3, 2))

            def ada_piece(g, slot):
                if isinstance(g, int) and g >= ADA_PIECES:
                    return
                if not isinstance(g, int) or g >= 2:
                    sp.wait_ge(ada_used, g)
                sp.dma_start(ada_ring[:, slot, :], ada[g]).then_inc(s_ada[slot], 16)

            def ada_ahead(phase, i, j):
                for n in range(sum(ADA_AT[phase][:j]), sum(ADA_AT[phase][:j + 1])):
                    ada_piece(KT // ADA[phase][1] * i + (ADA_G0[phase] + n + 2), n % 2)

            for g in range(2):
                ada_piece(g, g)

            def fox(i):
                for j in range(4):
                    load("fox", i, j)
                    ada_ahead("fox", i, j)

            loop(sp, "fox", fox)
            for j in range(4):
                load("gate", 0, j)
            sp.wait_ge(conv_out, 1)
            sp.dma_start(pwt, pw).then_inc(s_pw, 16)

            sp.wait_ge(pw_full.sem, pw_full.at("pw", 0, 4))
            for j in range(2):
                sp.dma_start(stage1[:, j, :], xT[:, j, :]).then_inc(s_stage[j], 16)

            def out1(i):
                for j in range(2):
                    load("out1", i, j)
                    ada_ahead("out1", i, j)
                    sp.wait_ge(residual_tile.sem, residual_tile.at("out1", i, j + 1))
                    sp.dma_start(spill[2 * i + j], Y[:, 2 * i + j, :]).then_inc(s_store[j], 16)
                    if not (isinstance(i, int) and i == 7):
                        sp.dma_start(stage1[:, j, :], xT[:, 2 * i + (2 + j), :]).then_inc(s_stage[j], 16)

            loop(sp, "out1", out1, peel=1)

            def att(i):
                sp.wait_ge(bias_used.sem, bias_used.at("att", i, 0))
                sp.dma_start(bt[:, :], bias[i]).then_inc(s_bias, 16)
                for j in range(4):
                    load("att", i, j)

            sp.wait_ge(norm2_tiles.sem, norm2_tiles.at("norm2", 0, 1))
            loop(sp, "att", att)
            loop(sp, "hg", lambda i: [load("hg", i, j) for j in range(4)])
            for j in range(2):
                sp.wait_ge(s_store[j], 16 * 8)
            sp.wait_ge(query_decayed.sem, query_decayed.at("hg", 7, 1))
            for j in range(2):
                sp.dma_start(stage2[:, j, :], spill[j]).then_inc(s_stage[j], 16)

            def out2(i):
                for j in range(2):
                    load("out2", i, j)
                    sp.wait_ge(s_out, 2 * i + j + 1)
                    sp.dma_start(out[2 * i + j], wk[:, j, :]).then_inc(s_store[j], 16)
                    if not (isinstance(i, int) and i == 7):
                        sp.dma_start(stage2[:, j, :], spill[2 * i + (2 + j)]).then_inc(s_stage[j], 16)

            loop(sp, "out2", out2, peel=2)
            for j in range(2):
                sp.wait_ge(s_store[j], 16 * 16)

        @block.tensor
        def _(pe):
            mm = pe.matmul

            def project(phase, i, j, hi=act_hi, lo=act_lo, n=S, order=range(KT), hooks=None, use=None, part=None):
                s = slot(phase, j)
                pe.wait_ge(w_split, tile_no(phase, i, j) + 2)
                pe.wait_ge(evac[s], half(phase, i, j) + 1)
                for at, k in enumerate(order):
                    if part is not None:
                        pe.wait_ge(part, at + 1)
                    if use == "x":
                        pe.wait_ge(moving, 1 + at + 1)
                    elif use == "y":
                        pe.wait_ge(moving, 1 + KT + at + 1)
                    elif use == "h":
                        pe.wait_ge(h_odd, at // 2 + 1) if at % 2 else pe.wait_ge(moving, 1 + 2 * KT + at // 2 + 1)
                    elif use == "y2":
                        pe.wait_ge(moving, 1 + 2 * KT + KT // 2 + at + 1)
                    wh, wl = w_hi[:, s, k * P:(k + 1) * P], w_lo[:, s, k * P:(k + 1) * P]
                    o = ps_p[:, s, 0:n]
                    mm(o, wh, hi[:, k, 0:n], start=at == 0, stop=False)
                    mm(o, wh, lo[:, k, 0:n], start=False, stop=False)
                    last = mm(o, wl, hi[:, k, 0:n], start=False, stop=at == KT - 1)
                    if at == KT - 1:
                        last.then_inc(proj_done, 1)
                    if hooks and at in hooks:
                        hooks[at]()

            def side(phase, i, k, body):
                pe.wait_ge(side_free.sem, side_free.at(phase, i, k))
                body().then_inc(side_full.sem, 1)

            def turn_value(phase, i, k, src, n):
                def body():
                    pe.wait_ge(value_ready.sem, value_ready.at(phase, i, 1))
                    for t in range(n):
                        last = pe.transpose(ps_x[:, t * P:(t + 1) * P], src[:, t * P:(t + 1) * P], ident)
                    return last
                side(phase, i, k, body)

            pe.wait_ge(s_cols, 16)

            def mem_sum():
                pe.wait_ge(s_const, 32)
                pe.wait_ge(mem_added, KT)
                return mm(ps_x[:, 0:MEM], ones, ssq_b[:, 0:MEM], start=True, stop=True)

            def x_sum():
                pe.wait_ge(side_in.sem, side_in.at("xnorm", 0, 2))
                mm(ps_x[:, :], ones, ssq_a[:, :], start=True, stop=False)
                return mm(ps_x[:, :], ones, r1[:, :], start=False, stop=True)

            def mem(phase, i, first=None, second=None):
                hooks = {15: lambda: turn_value(phase, i, 0, wk[:, 3, :], MT)}
                project(phase, i, 0, mem_hi, mem_lo, MEM, hooks=first,
                        part=mem_split if phase == "mem_a" and i == 0 else None)
                project(phase, i, 1, mem_hi, mem_lo, MEM, hooks={**(second or {}), **hooks})

            def sum_rows(src, phase, i, k):
                def body():
                    pe.wait_ge(side_in.sem, side_in.at(phase, i, k + 1))
                    return mm(ps_x[:, :], ones, src, start=True, stop=True)
                return body

            mem("mem_a", 0, second={8: lambda: side("start", 0, 0, mem_sum)})
            mem("mem_a", 1)
            mem("mem_b", 0, first={14: lambda: side("xnorm", 0, 0, x_sum)})
            mem("mem_b", 1)
            loop(pe, "conv", lambda i: [project("conv", i, j, use="x" if isinstance(i, int) and i + j == 0 else None)
                                        for j in range(2)], head=1)
            project("flog", 0, 0)

            def scores(phase, i, t, q, k, mask):
                pe.wait_ge(qk_ready.sem, qk_ready.at(phase, i, 1))
                pe.wait_ge(scores_free.sem, scores_free.at(phase, i, max(t - 1, 0)))
                w = P * (t + 1)
                mm(ps_s[:, t % 2, 0:w], q[:, t * P:(t + 1) * P], k[:, 0:w], start=True, stop=False,
                   skip_group_check=True)
                mm(ps_s[:, t % 2, w - P:w], eye_b, mask, start=False, stop=True,
                   skip_group_check=True).then_inc(scores_full.sem, 1)

            def turn_probs(phase, i, j, pr):
                pe.wait_ge(probs_ready.sem, probs_ready.at(phase, i, 1))
                pe.wait_ge(probsT_ready.sem, probsT_ready.at(phase, i, max(j - 1, 0)))
                for t in range(j, QT):
                    last = pe.transpose(ps_t[:, j % 2, (t - j) * P:(t - j + 1) * P],
                                        pr[:, CAUSAL[t] + j * P:CAUSAL[t] + (j + 1) * P], ident)
                last.then_inc(probsT_full.sem, 1)

            def weigh(phase, i, k, v, pt):
                pe.wait_ge(heads_done.sem, heads_done.at(phase, i, 0))
                pe.wait_ge(side_free.sem, side_free.at(phase, i, k))
                for j in range(QT):
                    pe.wait_ge(probsT_ready.sem, probsT_ready.at(phase, i, j + 1))
                    last = mm(ps_o[:, j * P:S], v[:, j * P:(j + 1) * P], pt[:, CAUSAL_T[j]:CAUSAL_T[j] + S - j * P],
                              start=j == 0, stop=j == QT - 1, skip_group_check=True)
                last.then_inc(heads_full.sem, 1)

            def memh(i):
                def s2(b):
                    pe.wait_ge(qk_ready.sem, qk_ready.at("memh", i, 1))
                    pe.wait_ge(scores_free.sem, scores_free.at("memh", i, 0))
                    for t in (2 * b, 2 * b + 1):
                        last = mm(ps_s[:, b, (t % 2) * MEM:(t % 2 + 1) * MEM], qkv[:, 0, t * P:(t + 1) * P],
                                  mkv[:, 0, i, :], start=True, stop=True, skip_group_check=True)
                    last.then_inc(scores_full.sem, 1)

                def t2(j):
                    pe.wait_ge(probs_ready.sem, probs_ready.at("memh", i, 1))
                    pe.wait_ge(probsT_ready.sem, probsT_ready.at("memh", i, 0))
                    for t in range(QT):
                        last = pe.transpose(ps_t[:, j, t * P:(t + 1) * P],
                                            tp[:, 0, t * MEM + j * P:t * MEM + (j + 1) * P], ident)
                    last.then_inc(probsT_full.sem, 1)

                project("memh", i, 0)
                project("memh", i, 1, hooks={3: lambda: s2(0), 4: lambda: s2(1), 12: lambda: t2(0),
                                             13: lambda: t2(1)})
                pe.wait_ge(heads_done.sem, heads_done.at("memh", i, 0))
                pe.wait_ge(value_ready.sem, value_ready.at("memh", i, 1))
                for j in range(MT):
                    pe.wait_ge(probsT_ready.sem, probsT_ready.at("memh", i, j + 1))
                    last = mm(ps_o[:, :], qkv[:, 3, j * P:(j + 1) * P], tp[:, 1, j * S:(j + 1) * S],
                              start=j == 0, stop=j == MT - 1)
                last.then_inc(heads_full.sem, 1)
            loop(pe, "memh", memh)

            def c_columns():
                pe.wait_ge(side_in.sem, side_in.at("cums", 0, 1))
                for t in range(QT):
                    last = pe.transpose(ps_x[:, t * NFOX:(t + 1) * NFOX], cT[0:NFOX, t * P:(t + 1) * P],
                                        ident[0:NFOX, 0:NFOX])
                return last
            side("cums", 0, 0, c_columns)

            def ada_sum(phase, i, k):
                def body():
                    pe.wait_ge(side_in.sem, side_in.at(phase, i, k + 1))
                    for m in range(ADA[phase][0]):
                        last = mm(ps_x[:, m:m + 1], ada_acc[:, m * P:(m + 1) * P], one_c, start=True, stop=True)
                    return last
                return body

            def fox(i):
                def spread_c():
                    pe.wait_ge(side_in.sem, side_in.at("fox", i, 1))
                    return mm(ps_x[:, :], ones[0:NFOX, :], wk[0:NFOX, 0, :], start=True, stop=True)

                q, k, v = qkv[:, 0, :], qkv[:, 1, :], qkv[:, 2, :]
                project("fox", i, 0, hooks={7: lambda: side("fox", i, 0, spread_c)})
                project("fox", i, 1)
                project("fox", i, 2, hooks={7: lambda: scores("fox", i, 0, q, k, causal_b),
                                            8: lambda: scores("fox", i, 1, q, k, causal_b),
                                            10: lambda: scores("fox", i, 2, q, k, causal_b),
                                            13: lambda: scores("fox", i, 3, q, k, causal_b)})
                project("fox", i, 3, hooks={4: lambda: turn_value("fox", i, 1, v, QT),
                                            8: lambda: turn_probs("fox", i, 0, tp[:, 0, :]),
                                            9: lambda: turn_probs("fox", i, 1, tp[:, 0, :]),
                                            11: lambda: turn_probs("fox", i, 2, tp[:, 0, :]),
                                            12: lambda: turn_probs("fox", i, 3, tp[:, 0, :]),
                                            14: lambda: side("fox", i, 2, ada_sum("fox", i, 1))})
                weigh("fox", i, 2, qkv[:, 3, :], tp[:, 1, :])
            loop(pe, "fox", fox)

            def channel_sum(k):
                def body():
                    pe.wait_ge(side_in.sem, side_in.at("gate", 0, k + 1))
                    for c in range(NCONV):
                        last = mm(ps_x[:, :], ones, (Y[:, c, :], qkv[:, c, :])[k], start=c == 0, stop=c == NCONV - 1)
                    return last
                return lambda: side("gate", 0, k, body)
            project("gate", 0, 0, hooks={3: channel_sum(0)})
            project("gate", 0, 1, hooks={3: channel_sum(1)})
            project("gate", 0, 2)
            project("gate", 0, 3)

            def pointwise():
                pe.wait_ge(s_pw, 16)
                pe.wait_ge(pw_in.sem, pw_in.at("gate", 0, 1))
                for m in range(NCONV):
                    bank = (ps_s[:, 0, :], ps_s[:, 1, :], ps_t[:, 0, :], ps_t[:, 1, :])[m]
                    for c in range(NCONV):
                        last = mm(bank, pwt[:, c, m * P:(m + 1) * P], qkv[:, c, :], start=c == 0, stop=c == NCONV - 1)
                    last.then_inc(pw_full.sem, 1)

            late = [*range(4, KT), *range(4)]

            def out1(i):
                first = isinstance(i, int) and i == 0
                project("out1", i, 0, order=late, use="y", hooks={8: pointwise} if first else None)
                project("out1", i, 1, order=late, use="y",
                        hooks={14: lambda: side("out1", i, 0, ada_sum("out1", i, 0))})
            loop(pe, "out1", out1, head=1)

            def both_sums():
                pe.wait_ge(squares_added.sem, squares_added.at("out1", 7, 1))
                mm(ps_o[:, :], ones, ssq_b[:, :], start=True, stop=False)
                mm(ps_x[:, :], ones, ssq_a[:, :], start=True, stop=False)
                pe.wait_ge(squares_ready.sem, squares_ready.at("out1", 7, 4))
                mm(ps_o[:, :], ones, wk[:, 3, :], start=False, stop=True)
                return mm(ps_x[:, :], ones, wk[:, 1, :], start=False, stop=True)
            side("norm2", 0, 0, both_sums)

            def att(i):
                q, k, v = qkv2[:, 0, :], qkv2[:, 1, :], qkv2[:, 2, :]
                project("att", i, 0, use="h")
                project("att", i, 1, hooks={4: lambda: side("att", i, 0, sum_rows(wk[:, 0, :], "att", i, 0))})
                project("att", i, 2, hooks={4: lambda: side("att", i, 1, sum_rows(wk[:, 0, :], "att", i, 1)),
                                            10: lambda: scores("att", i, 0, q, k, chunk_b),
                                            11: lambda: scores("att", i, 1, q, k, chunk_b),
                                            14: lambda: scores("att", i, 2, q, k, chunk_b)})
                project("att", i, 3, hooks={1: lambda: scores("att", i, 3, q, k, chunk_b),
                                            4: lambda: turn_value("att", i, 2, v, QT),
                                            12: lambda: turn_probs("att", i, 0, tp2[:, 0, :]),
                                            13: lambda: turn_probs("att", i, 1, tp2[:, 0, :]),
                                            14: lambda: turn_probs("att", i, 2, tp2[:, 0, :]),
                                            15: lambda: turn_probs("att", i, 3, tp2[:, 0, :])})
                weigh("att", i, 3, qkv2[:, 3, :], tp2[:, 1, :])
            loop(pe, "att", att)

            def hg(i):
                def level(n):
                    def body():
                        pe.wait_ge(scores_free.sem, scores_free.at("hg", i, max(n - 1, 0)))
                        if n:
                            pe.wait_ge(level_in.sem, level_in.at("hg", i, n + 1))
                            left = right = hz[:, (n - 1) % 2, :]
                        else:
                            pe.wait_ge(query_ready.sem, query_ready.at("hg", i, 1))
                            left, right = hk, hq
                        for t in range(QT):
                            c = slice(t * P, (t + 1) * P)
                            moving, o = (right[:, c], ps_s[:, 0, c]) if n == 0 else (
                                right_halves(right[:, c], HALVES[n - 1]),
                                blocks(ps_s[:, n % 2, t * P // 2:(t + 1) * P // 2], HALVES[n - 1]))
                            last = mm(o, left[:, c], moving, start=True, stop=True, skip_group_check=True)
                        last.then_inc(scores_full.sem, 1)
                    return body

                def turn_keys():
                    pe.wait_ge(level_in.sem, level_in.at("hg", i, 1))
                    for t in range(QT):
                        last = pe.transpose(ps_x[:, t * P:(t + 1) * P], hkd[:, t * P:(t + 1) * P], ident)
                    return last

                def chunk_states():
                    pe.wait_ge(side_free.sem, side_free.at("hg", i, 2))
                    pe.wait_ge(states_ready.sem, states_ready.at("hg", i, 0))
                    for n in (0, 2, 4, 6, 1, 3, 5):
                        rows = slice(n % 2 * CHUNK, n % 2 * CHUNK + CHUNK)
                        last = mm(ps_t[:, n % 2, n // 2 * P:(n // 2 + 1) * P], hkn[rows, n // 2, :],
                                  hvn[rows, n // 2, :], start=True, stop=True, skip_group_check=True)
                        if n in (6, 5):
                            last.then_inc(kv_full.sem, 1)

                def within():
                    pe.wait_ge(heads_done.sem, heads_done.at("hg", i, 0))
                    pe.wait_ge(scores_masked.sem, scores_masked.at("hg", i, 1))
                    for t in range(QT):
                        mm(ps_o[:, t * P:(t + 1) * P], hvn[:, t, :], hA[:, t, :], start=t == 0, stop=False,
                           skip_group_check=True)

                def across():
                    pe.wait_ge(query_decayed.sem, query_decayed.at("hg", i, 1))
                    pe.wait_ge(states_ready.sem, states_ready.at("hg", i, 1))
                    for n in range(1, NCH):
                        c = slice(n * CHUNK, (n + 1) * CHUNK)
                        last = mm(ps_o[:, c], hS[:, n - 1, :], hqd[:, c], start=False, stop=n == NCH - 1,
                                  skip_group_check=True)
                    last.then_inc(heads_full.sem, 1)

                project("hg", i, 0)
                project("hg", i, 1, hooks={15: lambda: side("hg", i, 0, turn_keys)})
                project("hg", i, 2, hooks={8: level(0), 9: level(1), 11: level(2), 13: level(3), 15: level(4)})
                project("hg", i, 3, hooks={0: level(5), 2: level(6), 4: lambda: turn_value("hg", i, 1, hvT[:, :], QT),
                                           6: chunk_states, 9: within, 12: across})
                side("hg", i, 2, sum_rows(wk[:, 0, :], "hg", i, 0))
            loop(pe, "hg", hg)
            loop(pe, "out2", lambda i: [project("out2", i, j, use="y2") for j in range(2)])

        @block.scalar
        def _(act):
            o = Order(act, own["act"])
            fn = act.activation
            act.preload_act_table_set("natural_log_exp_and_others")

            def split(phase, i, j, ahead=1):
                t = tile_no(phase, i, j) + ahead
                if isinstance(t, int) and t >= NTILES:
                    return
                s = (TILE0[phase] + j + ahead) % 2
                act.wait_ge(s_raw[s], 16 * (half(phase, i, j + ahead) + 1))
                act.wait_ge(proj_done, t if not isinstance(t, int) else max(t, 1))
                fn(w_hi[:, s, :], raw[:, s, :], ACT.Copy).then_inc(w_hi_done, 1)

            def rows(dst, src, width, tmp):
                o.step(fn(tmp, src, ACT.Ln, scale=1.0 / width, bias=eps_c))
                o.settle()
                return fn(dst, tmp, ACT.Exp, scale=-0.5)

            def softplus(dst, src, bias=None):
                if bias is None:
                    o.step(fn(dst, src, ACT.Abs))
                else:
                    o.step(fn(dst, src, ACT.Abs, bias=bias))
                o.settle()
                o.step(fn(dst, dst, ACT.Exp, scale=-1.0))
                o.settle()
                return fn(dst, dst, ACT.Ln, bias=one_c[0:dst.shape[0], :])

            def sigmoid(phase, i, j, k, dst):
                act.wait_ge(proj_done, tile_no(phase, i, j) + 2)
                softplus(dst, ps_p[:, slot(phase, j), :]).then_inc(gate_soft.sem, 1)
                act.wait_ge(gate_log.sem, gate_log.at(phase, i, k))
                fn(dst, dst, ACT.Exp).then_inc(gate_sig.sem, 1)

            act.wait_ge(s_cols, 16)
            split("start", 0, 0, 0)
            for k in range(KT):
                if k % 4 == 0:
                    act.wait_ge(s_mem[k // 4], 16)
                fn(mem_hi[:, k, :], memv[:, k, :], ACT.Identity, scale=col("mem_norm_g", k)).then_inc(sqs, 1)

            def mem_rows():
                act.wait_ge(side_full.sem, side_full.at("start", 0, 1))
                rows(wk[:, 2, 0:MEM], ps_x[:, 0:MEM], D, ssq_b[:, 0:MEM]).then_inc(side_free.sem, 1)

            def x_squares(g):
                if g == 2:
                    act.wait_ge(mem_added, KT)
                for k in range(4 * g, 4 * g + 4):
                    if k % 4 == 0:
                        act.wait_ge(s_x[k // 4], 16)
                    n = (g - 2) % 4 * 4 + k % 4
                    if n >= 2:
                        act.wait_ge(sq_y if n % 2 else sq_x, n // 2)
                    fn(wk[:, n % 2, :], Y[:, k, :], ACT.Square).then_inc(sqs, 1)

            def x_hi(g):
                for k in range(4 * g, 4 * g + 4):
                    act.wait_ge(moving_hi, 2 + k)
                    fn(act_hi[:, k, :], x_ring[k % 3], ACT.Copy).then_inc(sqs, 1)

            def mem_tile(phase, i, j, extra):
                split(phase, i, j)
                extra()
                if j == 1:
                    act.wait_ge(side_full.sem, side_full.at(phase, i, 1))
                    h = (0 if phase == "mem_a" else 2) + i
                    fn(mkv[:, 1, h, :], ps_x[:, 0:MEM], ACT.Copy).then_inc(side_free.sem, 1)

            mem_tile("mem_a", 0, 0, lambda: (mem_rows(), x_squares(2)))
            mem_tile("mem_a", 0, 1, lambda: x_squares(3))
            mem_tile("mem_a", 1, 0, lambda: x_squares(0))
            mem_tile("mem_a", 1, 1, lambda: x_squares(1))

            def x_rows():
                act.wait_ge(side_full.sem, side_full.at("xnorm", 0, 1))
                rows(r1[:, :], ps_x[:, :], D, ssq_b[:, :]).then_inc(side_free.sem, 1)

            for n, (i, j) in enumerate(((0, 0), (0, 1), (1, 0), (1, 1))):
                mem_tile("mem_b", i, j, lambda: (n == 0 and x_rows(), x_hi(n)))

            def conv(i):
                split("conv", i, 0)
                act.wait_ge(evac[slot("conv", 1)], half("conv", i, 1) + 1)
                sigmoid("conv", i, 0, 1, wk[:, 0, :])
                split("conv", i, 1)
            loop(act, "conv", conv, order=o)

            o.settle()
            o.again()
            split("flog", 0, 0)
            act.wait_ge(evac[slot("conv", 1)], half("conv", 3, 1) + 2)
            act.wait_ge(proj_done, tile_no("flog", 0, 0) + 2)
            f8 = ps_p[0:NFOX, slot("flog", 0), :]
            b_f = cols[0:NFOX, COLS["b_f"][0]:COLS["b_f"][0] + 1]
            o.step(fn(wk[0:NFOX, 1, :], f8, ACT.Identity, bias=b_f))
            o.settle()
            softplus(wk[0:NFOX, 1, :], wk[0:NFOX, 1, :]).then_inc(gate_soft.sem, 1)
            act.sem_inc(gate_sig.sem, 1)
            act.wait_ge(conv_in, 1)
            fn(hcol[:, 3:5, :], hcol[:, 3:5, :], ACT.Exp).then_inc(lb_exp, 1)

            def gate_exp(phase, i, j, k=1, dst=0):
                act.wait_ge(heads_done.sem, heads_done.at(phase, i, 0))
                sigmoid(phase, i, j, k, wk[:, dst, :])

            def memh(i):
                split("memh", i, 0)
                split("memh", i, 1)
                act.wait_ge(heads_full.sem, heads_full.at("memh", i, 0))
                fn(qkv[:, 3, 0:MEM], mkv[:, 1, i, :], ACT.Copy).then_inc(value_ready.sem, 1)
                act.wait_ge(max_ready.sem, max_ready.at("memh", i, 1))
                for t in range(QT):
                    e = fn(tp[:, 0, t * MEM:(t + 1) * MEM], ps_s[:, t // 2, t % 2 * MEM:(t % 2 + 1) * MEM], ACT.Exp,
                           bias=stat[:, 1, t:t + 1], accum_out=stat[:, 2, t:t + 1])
                    if t % 2:
                        e.then_inc(scores_free.sem, 1)
                    else:
                        o.step(e)
                fn(stat[:, 4, 0:1], one_c, ACT.Copy).then_inc(exp_done.sem, 1)
                for j in range(MT):
                    act.wait_ge(probsT_full.sem, probsT_full.at("memh", i, j + 1))
                    fn(tp[:, 1, j * S:(j + 1) * S], ps_t[:, j, :], ACT.Copy).then_inc(probsT_ready.sem, 1)
                gate_exp("memh", i, 1)
            loop(act, "memh", memh, order=o)
            o.settle()
            o.again()
            act.wait_ge(side_full.sem, side_full.at("cums", 0, 1))
            fn(cn[:, :, :].rearrange("p t h -> p (t h)"), ps_x[:, 0:QT * NFOX], ACT.Copy).then_inc(side_free.sem, 1)
            softplus(c_act[:, :], col("c_2", 0, KT)).then_inc(gate_soft.sem, 1)
            act.wait_ge(gate_log.sem, gate_log.at("cums", 0, 1))
            fn(c_act[:, :], c_act[:, :], ACT.Exp).then_inc(gate_sig.sem, 1)

            def exps(phase, i, t, pr):
                act.wait_ge(max_ready.sem, max_ready.at(phase, i, t + 1))
                e = pr[:, CAUSAL[t]:CAUSAL[t] + P * (t + 1)]
                fn(e, e, ACT.Exp, bias=stat[:, 1, t:t + 1], accum_out=stat[:, 2, t:t + 1]).then_inc(exp_done.sem, 1)

            def probsT(phase, i, j, pt):
                act.wait_ge(probsT_full.sem, probsT_full.at(phase, i, j + 1))
                n = S - j * P
                fn(pt[:, CAUSAL_T[j]:CAUSAL_T[j] + n], ps_t[:, j % 2, 0:n], ACT.Copy).then_inc(probsT_ready.sem, 1)

            def value_out(phase, i, j, dst):
                act.wait_ge(proj_done, tile_no(phase, i, j) + 2)
                o.step(fn(dst, ps_p[:, slot(phase, j), :], ACT.Copy))
                o.settle()
                act.sem_inc(evac[slot(phase, j)], 1)
                act.sem_inc(value_ready.sem, 1)

            def value_turned(phase, i, k, dst):
                act.wait_ge(side_full.sem, side_full.at(phase, i, k))
                fn(dst, ps_x[:, :], ACT.Copy).then_inc(side_free.sem, 1)

            def fox(i):
                split("fox", i, 0)
                act.wait_ge(side_full.sem, side_full.at("fox", i, 1))
                fn(wk[:, 1, :], ps_x[:, :], ACT.Copy, scale=-1.0).then_inc(side_free.sem, 1)
                split("fox", i, 1)
                split("fox", i, 2)
                for t in range(QT):
                    exps("fox", i, t, tp[:, 0, :])
                value_out("fox", i, 2, qkv[:, 2, :])
                split("fox", i, 3)
                value_turned("fox", i, 2, qkv[:, 3, :])
                for j in range(QT):
                    probsT("fox", i, j, tp[:, 1, :])
                gate_exp("fox", i, 3, dst=2)
            loop(act, "fox", fox, order=o)

            o.settle()
            o.again()

            def conv_gate(j):
                if j:
                    act.wait_ge(evac[slot("gate", j - 1)], half("gate", 0, j - 1) + 2)
                sigmoid("gate", 0, j, j + 1, wk[:, 2, :])

            split("gate", 0, 0)
            act.wait_ge(ln_ready.sem, ln_ready.at("gate", 0, 1))
            for c in range(NCONV):
                e = fn(qkv[:, c, :], Y[:, c, :], ACT.Square)
                if c < NCONV - 1:
                    o.step(e)
                else:
                    e.then_inc(side_in.sem, 1)
            conv_gate(0)
            split("gate", 0, 1)
            act.wait_ge(side_full.sem, side_full.at("gate", 0, 2))
            rows(r1[:, :], ps_x[:, :], NCONV * P, ssq_b[:, :]).then_inc(side_free.sem, 1)
            conv_gate(1)
            split("gate", 0, 2)
            act.wait_ge(ln_ready.sem, ln_ready.at("gate", 0, 2))
            for c in range(NCONV):
                o.step(fn(Y[:, c, :], Y[:, c, :], ACT.Identity, scale=col("conv_ln_g", c), bias=col("conv_ln_b", c)))
            o.settle()
            for c in range(NCONV + 1):
                if c < NCONV:
                    softplus(qkv[:, c, :], Y[:, c, :]).then_inc(ln_soft.sem, 1)
                if c:
                    act.wait_ge(ln_log.sem, ln_log.at("gate", 0, c))
                    fn(qkv[:, c - 1, :], qkv[:, c - 1, :], ACT.Exp).then_inc(ln_sig.sem, 1)
                if c == 2:
                    split("gate", 0, 3)
            conv_gate(2)

            def y_hi(order_):
                for k in order_:
                    fn(act_hi[:, k, :], Y[:, k, :], ACT.Copy).then_inc(moving_hi, 1)

            act.wait_ge(proj_done, tile_no("out1", 0, 0) + 1)
            act.wait_ge(heads_done.sem, heads_done.at("fox", 7, 1))
            y_hi(range(4, KT))
            conv_gate(3)
            split("out1", 0, 0)
            for m in range(NCONV):
                act.wait_ge(pw_done.sem, pw_done.at("pw", 0, m + 1))
                y_hi([m])

            def squares(i, j):
                act.wait_ge(residual_tile.sem, residual_tile.at("out1", i, j + 1))
                act.wait_ge(squares_added.sem, squares_added.at("out1", i, j))
                y, s = Y[:, 2 * i + j, :], j % 2
                fn(wk[:, s, :], y, ACT.Square).then_inc(squares_ready.sem, 1)
                fn(wk[:, 2 + s, :], y, ACT.Square,
                   scale=cols[:, bass.ds(2 * i + (COLS["final_g"][0] + j), 1)]).then_inc(squares_ready.sem, 1)

            def out1(i):
                if not (isinstance(i, int) and i == 0):
                    split("out1", i, 0)
                    squares(i, -1)
                split("out1", i, 1)
                squares(i, 0)
            loop(act, "out1", out1, head=1, order=o)
            squares(8, -1)
            o.settle()
            o.again()
            act.wait_ge(side_full.sem, side_full.at("norm2", 0, 1))
            rows(r1[:, :], ps_x[:, :], D, wk[:, 2, :]).then_inc(norm2_rows.sem, 1)
            act.wait_ge(norm2_mean.sem, norm2_mean.at("norm2", 0, 1))
            rows(wk[:, 2, :], wk[:, 3, :], D, wk[:, 2, :]).then_inc(norm2_rows.sem, 1)
            for k in range(KT):
                act.wait_ge(norm2_tiles.sem, norm2_tiles.at("norm2", 0, k + 1))
                h = h_ring[k % 2][k // 2 % 2]
                if k % 2 == 0:
                    fn(act_hi[:, k, :], h, ACT.Identity, bias=mod[:, k:k + 1]).then_inc(moving_hi, 1)
                else:
                    o.step(fn(h, h, ACT.Identity, bias=mod[:, k:k + 1]))
                    o.settle()
                    fn(act_hi[:, k, :], h, ACT.Copy).then_inc(h_full, 1)

            def att(i):
                def norm(j):
                    act.wait_ge(proj_done, tile_no("att", i, j) + 2)
                    if j == 0:
                        act.wait_ge(heads_done.sem, heads_done.at("att", i, 0))
                    fn(wk[:, 0, :], ps_p[:, slot("att", j), :], ACT.Square).then_inc(side_in.sem, 1)

                def norm_rows(j):
                    act.wait_ge(side_full.sem, side_full.at("att", i, j + 1))
                    o.step(fn(wk[:, 1, :], ps_x[:, :], ACT.Ln, scale=1.0 / P, bias=eps_c))
                    o.settle()
                    act.sem_inc(side_free.sem, 1)
                    fn(wk[:, 1, :], wk[:, 1, :], ACT.Exp, scale=-0.5).then_inc(rms_rows.sem, 1)

                split("att", i, 0)
                norm(0)
                split("att", i, 1)
                norm_rows(0)
                norm(1)
                split("att", i, 2)
                norm_rows(1)
                for t in range(3):
                    exps("att", i, t, tp2[:, 0, :])
                value_out("att", i, 2, qkv2[:, 2, :])
                split("att", i, 3)
                exps("att", i, 3, tp2[:, 0, :])
                value_turned("att", i, 3, qkv2[:, 3, :])
                for j in range(QT):
                    probsT("att", i, j, tp2[:, 1, :])
                gate_exp("att", i, 3, dst=2)
            loop(act, "att", att, order=o)

            def hg(i):
                split("hg", i, 0)
                act.wait_ge(proj_done, tile_no("hg", i, 0) + 2)
                softplus(wk[:, 1, :], ps_p[:, slot("hg", 0), :]).then_inc(gate_soft.sem, 1)
                split("hg", i, 1)
                act.wait_ge(gate_log.sem, gate_log.at("hg", i, 1))
                act.wait_ge(level_in.sem, level_in.at("hg", i, 0))
                act.wait_ge(scores_full.sem, scores_full.at("hg", i, 0))
                o.step(fn(wk[:, 0, :], wk[:, 0, :], ACT.Exp))
                fn(hk, wk[:, 1, :], ACT.Exp, scale=-1.0).then_inc(gate_sig.sem, 1)
                o.settle()
                fn(hd[:, 0, :], wk[:, 0, :], ACT.Ln, scale=hcol[:, 1, bass.ds(i, 1)],
                   bias=hcol[:, 2, bass.ds(i, 1)]).then_inc(forget_log.sem, 1)
                act.wait_ge(decay_ready.sem, decay_ready.at("hg", i, 1))
                fn(heb[:, :], hb[:, :], ACT.Exp).then_inc(decay_exp.sem, 1)

                def level_exp(n):
                    act.wait_ge(level_diff.sem, level_diff.at("hg", i, n + 1))
                    d = hd[:, n % 2, :]
                    if n:
                        o.step(fn(d, d, ACT.Abs))
                        o.settle()
                    fn(d, d, ACT.Exp, scale=-1.0).then_inc(level_exps.sem, 1)
                for n in range(3):
                    level_exp(n)
                sigmoid("hg", i, 1, 2, wk[:, 3, :])
                split("hg", i, 2)
                act.wait_ge(side_full.sem, side_full.at("hg", i, 1))
                fn(hkn[:, :, :].rearrange("p t d -> p (t d)"), ps_x[:, :], ACT.Copy).then_inc(side_free.sem, 1)
                for n in range(3, NLEV):
                    level_exp(n)
                value_out("hg", i, 2, hvT[:, :])
                split("hg", i, 3)
                value_turned("hg", i, 2, hvn[:, :, :].rearrange("p t d -> p (t d)"))
                act.wait_ge(heads_full.sem, heads_full.at("hg", i, 1))
                fn(wk[:, 0, :], ps_o[:, :], ACT.Square).then_inc(side_in.sem, 1)
                sigmoid("hg", i, 3, 3, wk[:, 2, :])
                act.wait_ge(side_full.sem, side_full.at("hg", i, 3))
                o.step(fn(ssq_a[:, :], ps_x[:, :], ACT.Ln, scale=1.0 / P, bias=eps_c))
                o.settle()
                act.sem_inc(side_free.sem, 1)
                fn(ssq_a[:, :], ssq_a[:, :], ACT.Exp, scale=-0.5).then_inc(rms_rows.sem, 1)
            loop(act, "hg", hg, order=o)
            act.wait_ge(proj_done, tile_no("out2", 0, 0) + 1)
            for k in range(KT):
                if k == KT - 1:
                    act.wait_ge(heads_done.sem, heads_done.at("hg", 7, 1))
                elif k == 0:
                    act.wait_ge(heads_done.sem, heads_done.at("hg", 7, 0))
                fn(act_hi[:, k, :], Y[:, k, :], ACT.Copy).then_inc(moving_hi, 1)

            def out2(i):
                split("out2", i, 0)
                split("out2", i, 1)
            loop(act, "out2", out2, peel=1)

        @block.vector
        def _(dve):
            o = Order(dve, own["dve"])
            tt, ts, stt = dve.tensor_tensor, dve.tensor_scalar, dve.scalar_tensor_tensor

            def do(ins):
                o.step(ins)
                o.settle()

            def split(phase, i, j, ahead=1):
                t = tile_no(phase, i, j) + ahead
                if isinstance(t, int) and t >= NTILES:
                    return
                s = (TILE0[phase] + j + ahead) % 2
                dve.wait_ge(w_hi_done, t + 2)
                tt(w_lo[:, s, :], raw[:, s, :], w_hi[:, s, :].bitcast(F32), ALU.subtract).then_inc(w_split, 1)

            def log_sigmoid(phase, i, j, k, dst):
                dve.wait_ge(gate_soft.sem, gate_soft.at(phase, i, k))
                stt(dst, ps_p[:, slot(phase, j), :], 0.0, dst, ALU.min, ALU.subtract).then_inc(gate_log.sem, 1)
                dve.wait_ge(gate_sig.sem, gate_sig.at(phase, i, k))

            dve.wait_ge(s_cols, 16)
            split("start", 0, 0, 0)

            def mem_add(k):
                dve.wait_ge(mem_sq, k + 1)
                sq = wk[:, (0, 1, 3)[k % 3], 0:MEM]
                if k == 0:
                    ins = dve.tensor_copy(ssq_b[:, 0:MEM], sq)
                else:
                    dve.wait_ge(mem_added, k)
                    ins = tt(ssq_b[:, 0:MEM], ssq_b[:, 0:MEM], sq, ALU.add)
                ins.then_inc(mem_added, 1)

            for k in range(KT):
                dve.wait_ge(s_mem[k // 4], 16)
                dve.wait_ge(sqs, k + 1)
                stt(mem_lo[:, k, :], memv[:, k, :], col("mem_norm_g", k), mem_hi[:, k, :].bitcast(F32), ALU.mult,
                    ALU.subtract).then_inc(mem_split, 1)
                if k % 2:
                    mem_add(k // 2)
            for k in range(KT // 2, 11):
                mem_add(k)

            def x_sums(g):
                for n in range((g - 2) % 4 * 4 + 1, (g - 2) % 4 * 4 + 4, 2):
                    dve.wait_ge(sqs, KT + n + 1)
                    if n == 1:
                        ins = dve.tensor_copy(r1[:, :], wk[:, 1, :])
                    else:
                        dve.wait_ge(sq_y, n // 2)
                        ins = tt(r1[:, :], r1[:, :], wk[:, 1, :], ALU.add)
                    ins.then_inc(sq_y if n < KT - 1 else side_in.sem, 1)

            def x_norm(g):
                if g == 0:
                    dve.wait_ge(side_free.sem, side_free.at("xnorm", 0, 1))
                for k in range(4 * g, 4 * g + 4):
                    if k >= 3:
                        dve.wait_ge(moving, 1 + k - 2)
                    stt(x_ring[k % 3], Y[:, k, :], col("norm_g", k), r1[:, :], ALU.mult, ALU.mult).then_inc(
                        moving_hi, 1)

            def mem_tile(phase, i, j, extra):
                split(phase, i, j)
                extra()
                s = slot(phase, j)
                norm = wk[:, 2, 0:MEM]
                dve.wait_ge(proj_done, tile_no(phase, i, j) + 2)
                if j == 0:
                    dve.wait_ge(side_free.sem, side_free.at("start", 0, 1))
                    dve.wait_ge(side_full.sem, side_full.at(phase, i, 0))
                    do(tt(wk[:, 3, 0:MEM], ps_p[:, s, 0:MEM], norm, ALU.mult))
                    dve.sem_inc(evac[s], 1)
                    dve.sem_inc(value_ready.sem, 1)
                else:
                    h = (0 if phase == "mem_a" else 2) + i
                    tt(mkv[:, 0, h, :], ps_p[:, s, 0:MEM], norm, ALU.mult).then_inc(evac[s], 1)

            mem_tile("mem_a", 0, 0, lambda: ([mem_add(k) for k in range(11, KT)], x_sums(2)))
            mem_tile("mem_a", 0, 1, lambda: x_sums(3))
            mem_tile("mem_a", 1, 0, lambda: x_sums(0))
            mem_tile("mem_a", 1, 1, lambda: x_sums(1))
            for n, (i, j) in enumerate(((0, 0), (0, 1), (1, 0), (1, 1))):
                mem_tile("mem_b", i, j, lambda: x_norm(n))
            dve.wait_ge(s_const, 32)
            dve.wait_ge(proj_done, TILE0["conv"] + 1)
            do(dve.memset(upad[:, :, 0:TAPS - 1], 0.0))
            l0, l1 = col("lower_bounds_2", 0, 8), col("lower_bounds_2", 8, 8)
            do(tt(hcol[:, 0, :], l0, l1, ALU.max))
            do(tt(hcol[:, 3, :], l0, hcol[:, 0, :], ALU.subtract))
            tt(hcol[:, 4, :], l1, hcol[:, 0, :], ALU.subtract).then_inc(conv_in, 1)

            def conv(i):
                s0, s1 = slot("conv", 0), slot("conv", 1)
                split("conv", i, 0)
                log_sigmoid("conv", i, 0, 1, wk[:, 0, :])
                dve.sem_inc(evac[s0], 1)
                split("conv", i, 1)
                dve.wait_ge(proj_done, tile_no("conv", i, 1) + 2)
                tt(upad[:, i, TAPS - 1:TAPS - 1 + S], ps_p[:, s1, :], wk[:, 0, :], ALU.mult).then_inc(evac[s1], 1)
            loop(dve, "conv", conv, order=o)

            o.settle()
            o.again()
            s = slot("flog", 0)
            dve.wait_ge(evac[slot("conv", 1)], half("conv", 3, 1) + 2)
            dve.sem_inc(conv_in, 1)
            split("flog", 0, 0)
            dve.wait_ge(gate_soft.sem, gate_soft.at("flog", 0, 1))
            do(ts(wk[0:NFOX, 2, :], ps_p[0:NFOX, s, :], cols[0:NFOX, COLS["b_f"][0]:COLS["b_f"][0] + 1], 0.0,
                  ALU.add, ALU.min))
            dve.sem_inc(evac[s], 1)
            dve.sem_inc(gate_log.sem, 1)
            do(tt(wk[0:NFOX, 2, :], wk[0:NFOX, 2, :], wk[0:NFOX, 1, :], ALU.subtract))
            do(dve.memset(wk[0:NFOX, 3, :], 1.0))
            dve.tensor_tensor_scan(cT[0:NFOX, :], wk[0:NFOX, 3, :], wk[0:NFOX, 2, :], 0.0, ALU.mult,
                                   ALU.add).then_inc(side_in.sem, 1)

            def silu_gate(phase, i, j, e, k=1):
                log_sigmoid(phase, i, j, k, e)
                do(tt(wk[:, 3, :], ps_p[:, slot(phase, j), :], e, ALU.mult))
                dve.sem_inc(evac[slot(phase, j)], 1)

            def memh(i):
                split("memh", i, 0)
                dve.wait_ge(proj_done, tile_no("memh", i, 0) + 2)
                dve.wait_ge(heads_full.sem, heads_full.at("memh", i, 0))
                do(ts(qkv[:, 0, :], ps_p[:, slot("memh", 0), :], SCALE, None, ALU.mult))
                dve.sem_inc(evac[slot("memh", 0)], 1)
                dve.sem_inc(qk_ready.sem, 1)
                split("memh", i, 1)
                for b in range(2):
                    dve.wait_ge(scores_full.sem, scores_full.at("memh", i, b + 1))
                    do(dve.reduce_max(stat[:, 0, 2 * b:2 * b + 2],
                                      ps_s[:, b, :].rearrange("p (t m) -> p t m", t=2), AX_X))
                ts(stat[:, 1, :], stat[:, 0, :], -1.0, None, ALU.mult).then_inc(max_ready.sem, 1)
                dve.wait_ge(exp_done.sem, exp_done.at("memh", i, 1))
                do(dve.reciprocal(stat[:, 3, :], stat[:, 2, :]))
                for t in range(QT):
                    e = tp[:, 0, t * MEM:(t + 1) * MEM]
                    ins = ts(e, e, stat[:, 3, t:t + 1], None, ALU.mult)
                    if t < QT - 1:
                        o.step(ins)
                    else:
                        ins.then_inc(probs_ready.sem, 1)
                silu_gate("memh", i, 1, wk[:, 0, :])
                dve.wait_ge(heads_full.sem, heads_full.at("memh", i, 1))
                tt(Y[:, 12 + i, :], ps_o[:, :], wk[:, 3, :], ALU.mult).then_inc(heads_done.sem, 1)
            loop(dve, "memh", memh, order=o)
            o.settle()
            o.again()

            def soft_in(phase, i, t, add):
                dve.wait_ge(scores_full.sem, scores_full.at(phase, i, t + 1))
                pr = (tp if phase == "fox" else tp2)[:, 0, :]
                e = pr[:, CAUSAL[t]:CAUSAL[t] + P * (t + 1)]
                add(t, e).then_inc(scores_free.sem, 1)
                dve.wait_ge(scores_free.sem, scores_free.at(phase, i, t + 1))
                do(dve.reduce_max(stat[:, 0, t:t + 1], e, AX_X))
                ts(stat[:, 1, t:t + 1], stat[:, 0, t:t + 1], -1.0, None, ALU.mult).then_inc(max_ready.sem, 1)

            def soft_out(phase, i, t):
                dve.wait_ge(exp_done.sem, exp_done.at(phase, i, t + 1))
                do(dve.reciprocal(stat[:, 3, t:t + 1], stat[:, 2, t:t + 1]))
                pr = (tp if phase == "fox" else tp2)[:, 0, :]
                e = pr[:, CAUSAL[t]:CAUSAL[t] + P * (t + 1)]
                ins = ts(e, e, stat[:, 3, t:t + 1], None, ALU.mult)
                if t < QT - 1:
                    o.step(ins)
                else:
                    ins.then_inc(probs_ready.sem, 1)

            dve.wait_ge(side_free.sem, side_free.at("cums", 0, 1))
            dve.wait_ge(gate_soft.sem, gate_soft.at("cums", 0, 1))
            stt(c_act[:, :], col("c_2", 0, KT), 0.0, c_act[:, :], ALU.min, ALU.subtract).then_inc(gate_log.sem, 1)
            dve.wait_ge(gate_sig.sem, gate_sig.at("cums", 0, 1))
            do(tt(c_act[:, :], c_act[:, :], col("c_2", 0, KT), ALU.mult))
            dve.sem_inc(ada_used, 1)

            def ada_step(phase, i, j):
                cols_n, kts = ADA[phase]
                per, g0, width = KT // kts, ADA_G0[phase], cols_n * P
                acc = ada_acc[:, 0:width]
                for n in range(sum(ADA_AT[phase][:j]), sum(ADA_AT[phase][:j + 1])):
                    s = n % 2
                    dve.wait_ge(s_ada[s], 8 * per * i + 16 * ((g0 + n) // 2 + 1))
                    for m in range(kts):
                        w, c = ada_ring[:, s, m * width:(m + 1) * width], c_act[:, n * kts + m:n * kts + m + 1]
                        if n == 0 and m == 0:
                            dve.wait_ge(side_full.sem, side_full.at(phase, i, 0))
                            ins = ts(acc, w, c, None, ALU.mult)
                        else:
                            ins = stt(acc, w, c, acc, ALU.mult, ALU.add)
                        if m < kts - 1:
                            do(ins)
                        else:
                            ins.then_inc(ada_used, 1)
                            dve.wait_ge(ada_used, per * i + (g0 + n + 2))
                    if n == per - 1:
                        dve.sem_inc(side_in.sem, 1)

            def ada_out(phase, i, k):
                n, m0 = ADA[phase][0], ADA_M0[phase]
                dve.wait_ge(side_full.sem, side_full.at(phase, i, k))
                tt(mod[:, bass.ds(n * i + m0, n)], ps_x[:, 0:n],
                   cols[:, bass.ds(n * i + (COLS["b_ada_2"][0] + m0), n)], ALU.add).then_inc(side_free.sem, 1)

            def fox(i):
                ts(wk[0:NFOX, 0, :], cT[0:NFOX, :], ident[0:NFOX, bass.ds(i, 1)], None, ALU.mult).then_inc(side_in.sem, 1)
                split("fox", i, 0)
                ada_step("fox", i, 0)
                dve.wait_ge(proj_done, tile_no("fox", i, 0) + 2)
                do(ts(qkv[:, 0, :], ps_p[:, slot("fox", 0), :], SCALE, None, ALU.mult))
                dve.sem_inc(evac[slot("fox", 0)], 1)
                split("fox", i, 1)
                ada_step("fox", i, 1)
                dve.wait_ge(proj_done, tile_no("fox", i, 1) + 2)
                do(dve.tensor_copy(qkv[:, 1, :], ps_p[:, slot("fox", 1), :]))
                dve.sem_inc(evac[slot("fox", 1)], 1)
                dve.sem_inc(qk_ready.sem, 1)
                split("fox", i, 2)
                dve.wait_ge(side_free.sem, side_free.at("fox", i, 1))
                for t in range(QT):
                    soft_in("fox", i, t, lambda t, e: stt(e, wk[:, 1, 0:P * (t + 1)], cn[:, t, bass.ds(i, 1)],
                                                          ps_s[:, t % 2, 0:P * (t + 1)], ALU.add, ALU.add))
                for t in range(QT):
                    soft_out("fox", i, t)
                split("fox", i, 3)
                ada_step("fox", i, 3)
                ada_out("fox", i, 3)
                silu_gate("fox", i, 3, wk[:, 2, :])
                dve.wait_ge(heads_full.sem, heads_full.at("fox", i, 1))
                tt(Y[:, 4 + i, :], ps_o[:, :], wk[:, 3, :], ALU.mult).then_inc(heads_done.sem, 1)
            loop(dve, "fox", fox, order=o)

            o.settle()
            o.again()
            dve.wait_ge(conv_out, 1)

            def conv_gate(j):
                log_sigmoid("gate", 0, j, j + 1, wk[:, 2, :])
                tt(tp[:, :, :].rearrange("p a n -> p (a n)")[:, j * S:(j + 1) * S], ps_p[:, slot("gate", j), :],
                   wk[:, 2, :], ALU.mult).then_inc(evac[slot("gate", j)], 1)
                dve.wait_ge(evac[slot("gate", j)], half("gate", 0, j) + 2)

            dve.sem_inc(side_in.sem, 1)
            split("gate", 0, 0)
            dve.wait_ge(side_full.sem, side_full.at("gate", 0, 1))
            do(ts(ssq_b[:, :], ps_x[:, :], 1.0 / (NCONV * P), None, ALU.mult))
            dve.sem_inc(side_free.sem, 1)
            for c in range(NCONV):
                o.step(tt(Y[:, c, :], Y[:, c, :], ssq_b[:, :], ALU.subtract))
            o.settle()
            dve.sem_inc(ln_ready.sem, 1)
            conv_gate(0)
            split("gate", 0, 1)
            dve.wait_ge(side_free.sem, side_free.at("gate", 0, 2))
            for c in range(NCONV):
                o.step(tt(Y[:, c, :], Y[:, c, :], r1[:, :], ALU.mult))
            o.settle()
            dve.sem_inc(ln_ready.sem, 1)
            conv_gate(1)
            split("gate", 0, 2)
            for c in range(NCONV + 1):
                if c < NCONV:
                    dve.wait_ge(ln_soft.sem, ln_soft.at("gate", 0, c + 1))
                    stt(qkv[:, c, :], Y[:, c, :], 0.0, qkv[:, c, :], ALU.min, ALU.subtract).then_inc(ln_log.sem, 1)
                if c:
                    dve.wait_ge(ln_sig.sem, ln_sig.at("gate", 0, c))
                    o.step(tt(qkv[:, c - 1, :], qkv[:, c - 1, :], Y[:, c - 1, :], ALU.mult))
                if c == 2:
                    split("gate", 0, 3)
            o.settle()
            dve.sem_inc(pw_in.sem, 1)
            conv_gate(2)

            lows = [0]

            def y_lo(order_):
                for k in order_:
                    lows[0] += 1
                    dve.wait_ge(moving_hi, 1 + KT + lows[0])
                    tt(act_lo[:, k, :], Y[:, k, :], act_hi[:, k, :].bitcast(F32), ALU.subtract).then_inc(moving, 1)

            y_lo(range(4, KT))
            conv_gate(3)
            split("out1", 0, 0)
            for m in range(NCONV):
                dve.wait_ge(pw_full.sem, pw_full.at("pw", 0, m + 1))
                bank = (ps_s[:, 0, :], ps_s[:, 1, :], ps_t[:, 0, :], ps_t[:, 1, :])[m]
                tt(Y[:, m, :], bank, tp[:, :, :].rearrange("p a n -> p (a n)")[:, m * S:(m + 1) * S],
                   ALU.mult).then_inc(pw_done.sem, 1)
                y_lo([m])
            do(dve.memset(ssq_a[:, :], 0.0))
            do(dve.memset(ssq_b[:, :], 0.0))
            dve.wait_ge(lb_exp, 1)
            do(tt(hcol[:, 5, :], hcol[:, 3, :], hcol[:, 4, :], ALU.add))
            do(dve.reciprocal(hcol[:, 5, :], hcol[:, 5, :]))
            do(tt(hcol[:, 0, :], hcol[:, 3, :], hcol[:, 5, :], ALU.mult))
            do(ts(hcol[:, 1, :], hcol[:, 0, :], -1.0, 1.0, ALU.mult, ALU.add))
            do(ts(hcol[:, 2, :], hcol[:, 0, :], LB_LEAST, None, ALU.max))
            do(ts(gall[:, :], mod[:, KT:2 * KT], 1.0, None, ALU.add))
            do(tt(gall[:, :], gall[:, :], col("norm_g_2", 0, KT), ALU.mult))
            do(tt(gall[:, :], gall[:, :], col("final_g", 0, KT), ALU.mult))
            do(ts(hcol[:, 6, 0:1], col("q_norm_g_2"), SCALE, None, ALU.mult))

            def out1(i):
                for j in range(2):
                    s = slot("out1", j)
                    if not (isinstance(i, int) and i + j == 0):
                        split("out1", i, j)
                    ada_step("out1", i, j)
                    dve.wait_ge(proj_done, tile_no("out1", i, j) + 2)
                    dve.wait_ge(s_stage[j], 16 * i + 16)
                    o.step(tt(Y[:, 2 * i + j, :], ps_p[:, s, :], stage1[:, j, :], ALU.add))
                    o.settle()
                    dve.sem_inc(evac[s], 1)
                    dve.sem_inc(residual_tile.sem, 1)
                ada_out("out1", i, 1)
            loop(dve, "out1", out1, head=1, order=o)
            o.settle()
            o.again()
            dve.wait_ge(norm2_rows.sem, norm2_rows.at("norm2", 0, 1))
            do(tt(wk[:, 3, :], ps_o[:, :], r1[:, :], ALU.mult))
            dve.sem_inc(side_free.sem, 1)
            tt(wk[:, 3, :], wk[:, 3, :], r1[:, :], ALU.mult).then_inc(norm2_mean.sem, 1)
            dve.wait_ge(norm2_rows.sem, norm2_rows.at("norm2", 0, 2))
            do(tt(wk[:, 2, :], wk[:, 2, :], r1[:, :], ALU.mult))

            def h_lo(k):
                dve.wait_ge(moving_hi, 1 + 2 * KT + k // 2 + 1)
                stt(act_lo[:, k, :], h_ring[0][k // 2 % 2], mod[:, k:k + 1], act_hi[:, k, :].bitcast(F32), ALU.add,
                    ALU.subtract).then_inc(moving, 1)

            for k in range(KT):
                if k >= 4:
                    dve.wait_ge(h_odd, k // 2 - 1) if k % 2 else dve.wait_ge(moving, 1 + 2 * KT + k // 2 - 1)
                stt(h_ring[k % 2][k // 2 % 2], Y[:, k, :], gall[:, k:k + 1], wk[:, 2, :], ALU.mult, ALU.mult).then_inc(
                    norm2_tiles.sem, 1)
                if k % 2:
                    h_lo(k - 1)
            for j in range(2):
                dve.wait_ge(s_store[j], 16 * 8)

            def att(i):
                def normed(j, gcol):
                    dve.wait_ge(rms_rows.sem, rms_rows.at("att", i, j + 1))
                    s = slot("att", j)
                    do(stt(qkv2[:, j, :], ps_p[:, s, :], gcol, wk[:, 1, :], ALU.mult, ALU.mult))
                    dve.sem_inc(evac[s], 1)
                    if j:
                        dve.sem_inc(qk_ready.sem, 1)

                def add_bias(t, e):
                    w = P * (t + 1)
                    n = min(w, 2 * P)
                    if w > n:
                        o.step(ts(e[:, 0:w - n], ps_s[:, t % 2, 0:w - n], bt[:, 2 * P:2 * P + 1], None, ALU.add))
                    return tt(e[:, w - n:w], ps_s[:, t % 2, w - n:w], bt[:, 2 * P - n:2 * P], ALU.add)

                split("att", i, 0)
                split("att", i, 1)
                normed(0, hcol[:, 6, 0:1])
                split("att", i, 2)
                normed(1, col("k_norm_g_2"))
                dve.wait_ge(s_bias, 16 * i + 16)
                for t in range(3):
                    soft_in("att", i, t, add_bias)
                for t in range(2):
                    soft_out("att", i, t)
                split("att", i, 3)
                soft_in("att", i, 3, add_bias)
                dve.wait_ge(max_ready.sem, max_ready.at("att", i, 4))
                dve.sem_inc(bias_used.sem, 1)
                for t in range(2, QT):
                    soft_out("att", i, t)
                silu_gate("att", i, 3, wk[:, 2, :])
                dve.wait_ge(heads_full.sem, heads_full.at("att", i, 1))
                tt(Y[:, i, :], ps_o[:, :], wk[:, 3, :], ALU.mult).then_inc(heads_done.sem, 1)
            loop(dve, "att", att, order=o)
            o.settle()
            o.again()
            do(dve.memset(hA[:, :, :], 0.0))

            def hg(i):
                s = slot("hg", 0)
                split("hg", i, 0)
                dve.wait_ge(gate_soft.sem, gate_soft.at("hg", i, 1))
                o.step(stt(wk[:, 0, :], ps_p[:, s, :], 0.0, wk[:, 1, :], ALU.min, ALU.subtract))
                o.step(stt(wk[:, 1, :], ps_p[:, s, :], 0.0, wk[:, 1, :], ALU.max, ALU.add))
                o.settle()
                dve.sem_inc(evac[s], 1)
                dve.sem_inc(gate_log.sem, 1)
                split("hg", i, 1)
                dve.wait_ge(gate_sig.sem, gate_sig.at("hg", i, 1))
                do(ts(hk, hk, hcol[:, 1, bass.ds(i, 1)], None, ALU.mult))
                dve.wait_ge(forget_log.sem, forget_log.at("hg", i, 1))
                dve.tensor_tensor_scan(hb[:, :], starts, hd[:, 0, :], 0.0, ALU.mult, ALU.add).then_inc(decay_ready.sem, 1)
                dve.wait_ge(decay_ready.sem, decay_ready.at("hg", i, 1))

                def diff(n):
                    width, ref = (CHUNK, CHUNK - 1) if n == 0 else (2 * HALVES[n - 1], HALVES[n - 1] - 1)
                    if n >= 2:
                        dve.wait_ge(level_in.sem, level_in.at("hg", i, n - 1))
                    b = blocks(hb[:, :], width)
                    r = b[:, :, ref:ref + 1].broadcast_to([P, S // width, width])
                    tt(blocks(hd[:, n % 2, :], width), b, r, ALU.subtract).then_inc(level_diff.sem, 1)

                for n in range(3):
                    diff(n)
                log_sigmoid("hg", i, 1, 2, wk[:, 3, :])
                s = slot("hg", 1)
                o.step(tt(hq[:, :], ps_p[:, s, :], wk[:, 3, :], ALU.mult))
                o.settle()
                dve.sem_inc(evac[s], 1)
                dve.sem_inc(query_ready.sem, 1)

                def masked(n):
                    dve.wait_ge(scores_full.sem, scores_full.at("hg", i, n + 1))
                    o.note()
                    o.settle()
                    a, mask, b = hA[:, :, :], levels[:, n:n + 1, :], ps_s[:, 0, :].rearrange("p (t n) -> p t n", t=QT)
                    if n:
                        h = HALVES[n - 1]
                        a, mask = right_halves(a, h), right_halves(mask, h)
                        b = ps_s[:, n % 2, 0:S // 2].rearrange("p (t b n) -> p t b n", t=QT, n=h)
                    dve.copy_predicated(a, mask.broadcast_to(list(a.shape)), b).then_inc(scores_free.sem, 1)
                    dve.wait_ge(scores_free.sem, scores_free.at("hg", i, n + 1))
                masked(0)
                for n in range(3, NLEV):
                    diff(n)
                    if n == 4:
                        split("hg", i, 2)
                    masked(n - 2)
                masked(NLEV - 2)
                masked(NLEV - 1)
                dve.sem_inc(scores_masked.sem, 1)
                split("hg", i, 3)
                dve.wait_ge(decay_exp.sem, decay_exp.at("hg", i, 1))
                dve.wait_ge(kv_full.sem, kv_full.at("hg", i, 1))
                do(dve.tensor_copy(hS[:, 0, :], ps_t[:, 0, 0:P]))
                for n in range(1, NCH - 1):
                    if n == 1:
                        dve.wait_ge(kv_full.sem, kv_full.at("hg", i, 2))
                    last = n * CHUNK + CHUNK - 1
                    do(stt(hS[:, n, :], hS[:, n - 1, :], heb[:, last:last + 1],
                           ps_t[:, n % 2, n // 2 * P:(n // 2 + 1) * P], ALU.mult, ALU.add))
                dve.sem_inc(states_ready.sem, 1)
                silu_gate("hg", i, 3, wk[:, 2, :], 3)
                dve.wait_ge(rms_rows.sem, rms_rows.at("hg", i, 1))
                do(stt(wk[:, 2, :], ps_o[:, :], col("hg_norm_g_2"), ssq_a[:, :], ALU.mult, ALU.mult))
                tt(Y[:, 8 + i, :], wk[:, 2, :], wk[:, 3, :], ALU.mult).then_inc(heads_done.sem, 1)
                dve.wait_ge(heads_done.sem, heads_done.at("hg", i, 1))
            loop(dve, "hg", hg, order=o)
            o.settle()
            o.again()
            for k in range(KT):
                dve.wait_ge(moving_hi, 1 + 2 * KT + KT // 2 + k + 1)
                tt(act_lo[:, k, :], Y[:, k, :], act_hi[:, k, :].bitcast(F32), ALU.subtract).then_inc(moving, 1)

            def out2(i):
                for j in range(2):
                    s = slot("out2", j)
                    split("out2", i, j)
                    dve.wait_ge(s_stage[j], 16 * 8 + 16 * i + 16)
                    dve.wait_ge(s_store[j], 16 * 8 + 16 * i)
                    do(stt(wk[:, j, :], stage2[:, j, :], cols[:, bass.ds(2 * i + (COLS["final_g"][0] + j), 1)], r1[:, :],
                           ALU.mult, ALU.mult))
                    dve.wait_ge(proj_done, tile_no("out2", i, j) + 2)
                    o.step(stt(wk[:, j, :], ps_p[:, s, :], mod[:, bass.ds(2 * i + (2 * KT + j), 1)], wk[:, j, :],
                               ALU.mult, ALU.add))
                    o.settle()
                    dve.sem_inc(evac[s], 1)
                    dve.sem_inc(s_out, 1)
            loop(dve, "out2", out2, peel=1, order=o)

        @block.gpsimd
        def _(pool):
            o = Order(pool, own["pool"])
            tt = pool.tensor_tensor
            pool.wait_ge(s_cols, 16)
            for k in range(KT):
                if k % 4 == 0:
                    pool.wait_ge(s_mem[k // 4], 16)
                if k >= 3:
                    pool.wait_ge(mem_added, k - 2)
                tt(wk[:, (0, 1, 3)[k % 3], 0:MEM], memv[:, k, :], memv[:, k, :], ALU.mult).then_inc(mem_sq, 1)
            for n in range(0, KT, 2):
                pool.wait_ge(sqs, KT + n + 1)
                if n == 0:
                    ins = pool.tensor_copy(ssq_a[:, :], wk[:, 0, :])
                else:
                    pool.wait_ge(sq_x, n // 2)
                    ins = tt(ssq_a[:, :], ssq_a[:, :], wk[:, 0, :], ALU.add)
                ins.then_inc(sq_x if n < KT - 2 else side_in.sem, 1)
            for k in range(KT):
                pool.wait_ge(sqs, 2 * KT + k + 1)
                tt(act_lo[:, k, :], x_ring[k % 3], act_hi[:, k, :].bitcast(F32), ALU.subtract).then_inc(moving, 1)
            pool.wait_ge(conv_in, 2)
            for c in range(NCONV):
                o.step(pool.tensor_copy(Y[:, c, :], col("conv_b", c).broadcast_to([P, S])))
            o.settle()
            with pool.Fori(0, TAPS) as tap:
                o.again()
                for c in range(NCONV):
                    w0 = COLS["conv_w"][0] + c * TAPS
                    o.step(tt(ctmp[:, :], upad[:, c, bass.ds(tap, S)],
                              cols[:, bass.ds(tap + w0, 1)].broadcast_to([P, S]), ALU.mult))
                    o.settle()
                    o.step(tt(Y[:, c, :], Y[:, c, :], ctmp[:, :], ALU.add))
                    o.settle()
            pool.sem_inc(conv_out, 1)

            def out1(i):
                for j in range(1 if isinstance(i, int) and i == 7 else 2):
                    pool.wait_ge(squares_ready.sem, squares_ready.at("out1", i, 2 * j + 2))
                    o.step(tt(ssq_a[:, :], ssq_a[:, :], wk[:, j, :], ALU.add))
                    o.step(tt(ssq_b[:, :], ssq_b[:, :], wk[:, 2 + j, :], ALU.add))
                    o.settle()
                    pool.sem_inc(squares_added.sem, 1)
            loop(pool, "out1", out1, peel=1, order=o)
            for n in range(KT // 2):
                pool.wait_ge(h_full, n + 1)
                tt(act_lo[:, 2 * n + 1, :], h_ring[1][n % 2], act_hi[:, 2 * n + 1, :].bitcast(F32),
                   ALU.subtract).then_inc(h_odd, 1)

            def hg(i):
                for n in range(NLEV):
                    pool.wait_ge(level_exps.sem, level_exps.at("hg", i, n + 1))
                    if n == 0:
                        pool.wait_ge(side_full.sem, side_full.at("hg", i, 0))
                        o.step(tt(hkd[:, :], hk[:, :], hd[:, 0, :], ALU.mult))
                        o.settle()
                        pool.sem_inc(level_in.sem, 1)
                        pool.wait_ge(query_ready.sem, query_ready.at("hg", i, 1))
                        continue
                    h = HALVES[n - 1]
                    if n >= 3:
                        pool.wait_ge(scores_full.sem, scores_full.at("hg", i, n - 1))
                    z = hz[:, (n - 1) % 2, :].rearrange("p (b n) -> p b n", n=2 * h)
                    d = hd[:, n % 2, :].rearrange("p (b n) -> p b n", n=2 * h)
                    k = hk[:, :].rearrange("p (b n) -> p b n", n=2 * h)
                    q = hq[:, :].rearrange("p (b n) -> p b n", n=2 * h)
                    o.step(tt(z[:, :, 0:h], k[:, :, 0:h], d[:, :, 0:h], ALU.mult))
                    tt(z[:, :, h:2 * h], q[:, :, h:2 * h], d[:, :, h:2 * h], ALU.mult).then_inc(level_in.sem, 1)
                pool.wait_ge(decay_exp.sem, decay_exp.at("hg", i, 1))
                pool.wait_ge(heads_full.sem, heads_full.at("hg", i, 0))
                tt(hqd[:, :], hq[:, :], heb[:, :], ALU.mult).then_inc(query_decayed.sem, 1)
            loop(pool, "hg", hg, order=o)
            pool.wait_ge(level_in.sem, level_in.at("hg", 7, 7))


def _tiles(np, w, starts):
    out = np.zeros((len(starts), P, KT, P), np.float32)
    for n, s in enumerate(starts):
        c = w[:, s:min(s + P, w.shape[1])] if not isinstance(s, tuple) else w[:, s[0]:s[1]]
        out[n, :, :, :c.shape[1]] = c.reshape(KT, P, c.shape[1]).transpose(1, 0, 2)
    return out.reshape(len(starts), P, D)


def kernel(**inputs):
    import numpy as np
    import concourse.bacc as _bacc
    from concourse import mybir as _mybir
    from concourse.bass_utils import run_bass_kernel_spmd as _run

    a = {k: np.asarray(v) for k, v in inputs.items()}
    w1, wkv, wo1 = a["w_in"][0], a["w_mem_kv"][0], a["w_out"][0]
    w2, wo2 = a["w_in_2"][0], a["w_out_2"][0]
    CW, FW = NCONV * P, NFOX * P
    fq, fk, fv, fl = 3 * CW, 3 * CW + FW, 3 * CW + 2 * FW, 3 * CW + 3 * FW
    fg, mq = fl + NFOX, fl + NFOX + FW
    mg = mq + NMEMH * P
    mv = NMEMH * P
    first = [t for i in range(4) for t in (CW + i * P, i * P)]
    first += [(fl, fl + NFOX)]
    first += [t for h in range(NMEMH) for t in (mq + h * P, mg + h * P)]
    first += [t for h in range(NFOX) for t in (fq + h * P, fk + h * P, fv + h * P, fg + h * P)]
    first += [2 * CW + i * P for i in range(4)]
    AW = NATT * P
    second = [t + h * P for h in range(NATT) for t in (0, AW, 2 * AW, 3 * AW)]
    second += [t + h * P for h in range(NHG) for t in (5 * AW, 4 * AW, 6 * AW, 7 * AW)]
    wt = np.concatenate([
        _tiles(np, wkv, [t for h in range(NMEMH) for t in (mv + h * P, h * P)]),
        _tiles(np, w1, first), _tiles(np, wo1, [m * P for m in range(KT)]),
        _tiles(np, w2, second), _tiles(np, wo2, [m * P for m in range(KT)])])
    assert wt.shape[0] == NTILES

    def along(v, n):
        return v.reshape(n, P).T

    cols = np.zeros((P, NCOLS), np.float32)

    def put(name, v):
        c, n = COLS[name]
        cols[:, c:c + n] = v
    for name in ("norm_g", "mem_norm_g", "norm_g_2", "c_2"):
        put(name, along(a[name][0], KT))
    put("final_g", along(a["final_g"], KT))
    put("b_ada_2", along(a["b_ada_2"][0], 48))
    put("conv_w", a["conv_w"][0].reshape(TAPS, NCONV, P).transpose(2, 1, 0).reshape(P, NCONV * TAPS))
    for name in ("conv_b", "conv_ln_g", "conv_ln_b"):
        put(name, along(a[name][0], NCONV))
    for name in ("q_norm_g_2", "k_norm_g_2", "hg_norm_g_2"):
        put(name, along(a[name][0], 1))
    put("lower_bounds_2", a["lower_bounds_2"].reshape(2, NHG, P).transpose(2, 0, 1).reshape(P, 2 * NHG))
    cols[0:NFOX, COLS["b_f"][0]] = a["b_f"][0]
    put("one", 1.0)
    put("eps", EPS)

    n = np.arange(P)
    consts = np.zeros((P, CONSTS), np.float32)
    consts[:, 0:P] = 1.0
    consts[:, P:2 * P] = np.eye(P)
    consts[:, 2 * P:] = (np.arange(S) % CHUNK != 0)[None, :]
    masks = np.zeros((P, 3 + NLEV, P), np.float32)
    masks[:, 0] = np.eye(P)
    masks[:, 1] = np.where(n[None, :] > n[:, None], NEG, 0.0)
    masks[:, 2] = np.where(n[None, :] // CHUNK > n[:, None] // CHUNK, NEG, 0.0)
    masks[:, 3] = np.eye(P)
    for m, h in enumerate(HALVES):
        s, t = n[:, None], n[None, :]
        masks[:, m + 4] = (s // (2 * h) == t // (2 * h)) & (s % (2 * h) < h) & (t % (2 * h) >= h)

    masks = masks.astype(_mybir.dt.np(BF16))

    rel = a["rel_bias_2"][0]
    dist = P + n[:, None] - np.arange(2 * P)[None, :]
    bias = np.empty((NATT, P, 2 * P + 1), np.float32)
    bias[:, :, 0:2 * P] = rel[:, np.minimum(dist, P) + P]
    bias[:, :, 2 * P] = rel[:, 2 * P][:, None]

    ada = []
    for phase, (c, r) in ADA.items():
        m0 = ADA_M0[phase] * P
        w = a["w_ada_2"][0][:, m0:m0 + 8 * c * P].reshape(KT // r, r, P, 8, c * P)
        ada.append(w.transpose(3, 0, 2, 1, 4).reshape(-1, P, ADA_PIECE))
    ada = np.concatenate(ada)
    assert ada.shape[0] == ADA_PIECES

    arrays = {
        "wt": wt,
        "ada": ada,
        "bias": bias,
        "xT": a["x"][0].T.reshape(KT, P, S).transpose(1, 0, 2),
        "memT": a["mem"][0].T.reshape(KT, P, MEM).transpose(1, 0, 2).reshape(P, KT // 2, S),
        "pw": a["w_conv_pw"][0].reshape(NCONV, P, CW).transpose(1, 0, 2),
        "cols": cols, "consts": consts, "masks": masks,
    }
    arrays = {f"{k}_dram": np.ascontiguousarray(v) for k, v in arrays.items()}
    nc = _bacc.Bacc("TRN2", target_bir_lowering=False, num_devices=1)
    args = [nc.dram_tensor(k, v.shape, _mybir.dt.from_np(v.dtype), kind="ExternalInput").ap()
            for k, v in arrays.items()]
    args.append(nc.dram_tensor("spill_dram", (KT, P, S), F32, kind="Internal").ap())
    args.append(nc.dram_tensor("out_dram", (KT, P, S), F32, kind="ExternalOutput").ap())
    build(nc, *args)
    r = _run(nc, [arrays], core_ids=[0])
    got = r.results[0]["out_dram"]
    return np.ascontiguousarray(np.asarray(got).reshape(D, S).T)[None]
```
